# Optimizing a Trainium2 kernel written in Bass

```python
import jax, jax.numpy as jnp
from jax import lax
import numpy as np
import math

D_MODEL = 1024
BATCH = 1
SEQ = 512
DEPTH = 2

N_A_LAYERS = DEPTH // 2
N_B_LAYERS = DEPTH - N_A_LAYERS
HGRN_EXPAND = 128
HGRN_HEADS = D_MODEL // HGRN_EXPAND
HGRN_DK = HGRN_EXPAND
HGRN_DV = D_MODEL // HGRN_HEADS
HGRN_D_KEY = HGRN_HEADS * HGRN_DK
HGRN_D_VAL = HGRN_HEADS * HGRN_DV
HGRN_CHUNK = 64
NSA_HEADS = 16
NSA_KV_HEADS = 4
NSA_GROUP = NSA_HEADS // NSA_KV_HEADS
NSA_HEAD_DIM = D_MODEL // NSA_HEADS
NSA_Q_WIDTH = NSA_HEADS * NSA_HEAD_DIM
N_BRANCH = 3
CMP_BLOCK = 32
CMP_STRIDE = 16
CMP_HIDDEN = 256
SEL_BLOCK = 64
N_SELECT = 16
WINDOW = 512
Q_BLOCK = 128
ROPE_THETA = 10000.0
FFN_HIDDEN = -(-8 * D_MODEL // (3 * 256)) * 256
EPS = 1e-6
NEG_INF = -1e30
FORCE_SCORE = 1e9


def rms_norm(x, gain):
    x32 = x.astype(jnp.float32)
    y = x32 * lax.rsqrt(jnp.mean(x32 * x32, axis=-1, keepdims=True) + EPS)
    return (y * gain.astype(jnp.float32)).astype(x.dtype)

def modulate(x, gain, shift, scale):
    return rms_norm(x, gain) * (1 + scale[:, None, :]) + shift[:, None, :]

def rope_tables(seq, dim):
    inv_freq = 1.0 / (ROPE_THETA ** (jnp.arange(0, dim, 2, dtype=jnp.float32) / dim))
    ang = jnp.arange(seq, dtype=jnp.float32)[:, None] * inv_freq[None, :]
    return jnp.cos(ang), jnp.sin(ang)

def apply_rope(x, cos, sin):
    x1, x2 = jnp.split(x, 2, axis=-1)
    cs = cos[None, :, None, :].astype(x.dtype)
    sn = sin[None, :, None, :].astype(x.dtype)
    return jnp.concatenate([x1 * cs - x2 * sn, x2 * cs + x1 * sn], axis=-1)

def masked_softmax(s, mask):
    p = jax.nn.softmax(jnp.where(mask, s.astype(jnp.float32), NEG_INF), axis=-1)
    return jnp.where(mask, p, 0.0)

def swiglu(h, w_in, w_out):
    a, b = jnp.split(h @ w_in, 2, axis=-1)
    return (jax.nn.silu(a) * b) @ w_out

def hgrn2_mixer(h, w_in, lower_bound, out_norm, w_out, first_layer):
    B, S, _ = h.shape
    q, f, i, g = jnp.split(h @ w_in, [HGRN_D_KEY, 2 * HGRN_D_KEY, 2 * HGRN_D_KEY + HGRN_D_VAL], axis=-1)
    q = jax.nn.silu(q)
    f32 = f.astype(jnp.float32)
    if first_layer:
        log_f = jax.nn.log_sigmoid(f32)
    else:
        lb = lower_bound.astype(jnp.float32)
        log_f = jnp.log(lb + (1.0 - lb) * jax.nn.sigmoid(f32))
    k = -jnp.expm1(log_f)
    nc = S // HGRN_CHUNK

    def to_chunks(t, d):
        return t.astype(jnp.float32).reshape(B, nc, HGRN_CHUNK, HGRN_HEADS, d).transpose(1, 0, 3, 2, 4)

    qc, kc, gc = to_chunks(q, HGRN_DK), to_chunks(k, HGRN_DK), to_chunks(log_f, HGRN_DK)
    vc = to_chunks(i, HGRN_DV)
    causal = jnp.tril(jnp.ones((HGRN_CHUNK, HGRN_CHUNK), dtype=bool))[:, :, None]

    def step(state, inp):
        q_, k_, v_, g_ = inp
        G = jnp.cumsum(g_, axis=2)
        o_inter = jnp.einsum('bhtk,bhkv->bhtv', q_ * jnp.exp(G), state)
        diff = G[:, :, :, None, :] - G[:, :, None, :, :]
        decay = jnp.where(causal, jnp.exp(jnp.where(causal, diff, 0.0)), 0.0)
        attn = jnp.einsum('bhtk,bhsk,bhtsk->bhts', q_, k_, decay)
        o_intra = jnp.einsum('bhts,bhsv->bhtv', attn, v_)
        G_last = G[:, :, -1:, :]
        new_state = jnp.exp(G_last[:, :, 0, :])[..., None] * state + jnp.einsum(
            'bhsk,bhsv->bhkv', k_ * jnp.exp(G_last - G), v_)
        return new_state, o_inter + o_intra

    s0 = jnp.zeros((B, HGRN_HEADS, HGRN_DK, HGRN_DV), jnp.float32)
    _, o = lax.scan(step, s0, (qc, kc, vc, gc))
    o = o.transpose(1, 0, 3, 2, 4).reshape(B, S, HGRN_HEADS, HGRN_DV)
    o = rms_norm(o, out_norm) * jax.nn.silu(g.reshape(B, S, HGRN_HEADS, HGRN_DV).astype(jnp.float32))
    return o.reshape(B, S, HGRN_D_VAL).astype(h.dtype) @ w_out

def nsa_shared_kv(h, w_kv, k_norm, cmp_pos, cmp_w1, cmp_w2, cos, sin):
    B, S, _ = h.shape
    kv = (h @ w_kv).reshape(B, S, 2 * N_BRANCH, NSA_KV_HEADS, NSA_HEAD_DIM)
    k_cmp, v_cmp, k_sel, v_sel, k_win, v_win = [kv[:, :, j] for j in range(2 * N_BRANCH)]
    n_sub = CMP_BLOCK // CMP_STRIDE
    n_cmp = S // CMP_STRIDE - n_sub + 1

    def compress(t, pos, w1, w2):
        r = t.reshape(B, S // CMP_STRIDE, CMP_STRIDE, NSA_KV_HEADS, NSA_HEAD_DIM)
        blocks = jnp.concatenate([r[:, j:j + n_cmp] for j in range(n_sub)], axis=2)
        blocks = blocks + pos[None, None, :, None, :]
        flat = blocks.transpose(0, 1, 3, 2, 4).reshape(B, n_cmp, NSA_KV_HEADS, CMP_BLOCK * NSA_HEAD_DIM)
        return jax.nn.silu(flat @ w1) @ w2

    kc = rms_norm(compress(k_cmp, cmp_pos[0], cmp_w1[0], cmp_w2[0]), k_norm[0])
    vc = compress(v_cmp, cmp_pos[1], cmp_w1[1], cmp_w2[1])
    n_sel = S // SEL_BLOCK
    ks = apply_rope(rms_norm(k_sel, k_norm[1]), cos, sin)
    ks_blocks = ks.reshape(B, n_sel, SEL_BLOCK, NSA_KV_HEADS, NSA_HEAD_DIM).transpose(0, 3, 1, 2, 4)
    vs_blocks = v_sel.reshape(B, n_sel, SEL_BLOCK, NSA_KV_HEADS, NSA_HEAD_DIM).transpose(0, 3, 1, 2, 4)
    kw = apply_rope(rms_norm(k_win, k_norm[2]), cos, sin)
    pad = ((0, 0), (WINDOW, 0), (0, 0), (0, 0))
    return (kc, vc, ks_blocks, vs_blocks, jnp.pad(kw, pad), jnp.pad(v_win, pad))

def nsa_mixer(h, w_q, q_norm, w_out, shared, cos, sin):
    B, S, _ = h.shape
    kc, vc, ks_blocks, vs_blocks, kw_pad, vw_pad = shared
    proj = h @ w_q
    q = rms_norm(proj[..., :NSA_Q_WIDTH].reshape(B, S, NSA_HEADS, NSA_HEAD_DIM), q_norm)
    gates = jax.nn.sigmoid(proj[..., NSA_Q_WIDTH:].astype(jnp.float32)).reshape(B, S, N_BRANCH, NSA_HEADS)
    q_rope = apply_rope(q, cos, sin)
    n_cmp = kc.shape[1]
    n_sel = ks_blocks.shape[2]
    n_top = min(N_SELECT, n_sel)
    cmp_end = jnp.arange(n_cmp) * CMP_STRIDE + CMP_BLOCK - 1
    sel_start = jnp.arange(n_sel) * SEL_BLOCK
    cs = np.arange(n_cmp) * CMP_STRIDE
    ss = np.arange(n_sel) * SEL_BLOCK
    overlap = jnp.asarray(((cs[:, None] < ss[None, :] + SEL_BLOCK) &
                           (cs[:, None] + CMP_BLOCK > ss[None, :])).astype(np.float32))
    scale = NSA_HEAD_DIM ** -0.5
    nb = S // Q_BLOCK
    bi = jnp.arange(B)[:, None, None, None]
    hi = jnp.arange(NSA_KV_HEADS)[None, :, None, None]
    blk_pos = jnp.arange(SEL_BLOCK)

    def blockify(t):
        return t.reshape(B, nb, Q_BLOCK, *t.shape[2:]).swapaxes(0, 1)

    def attend(args):
        blk, qp, qr, g = args
        t = blk * Q_BLOCK + jnp.arange(Q_BLOCK)
        qp = qp.reshape(B, Q_BLOCK, NSA_KV_HEADS, NSA_GROUP, NSA_HEAD_DIM)
        qr = qr.reshape(B, Q_BLOCK, NSA_KV_HEADS, NSA_GROUP, NSA_HEAD_DIM)
        s_c = jnp.einsum('bqhgd,bchd->bhgqc', qp, kc) * scale
        p_c = masked_softmax(s_c, cmp_end[None, :] <= t[:, None])
        o_c = jnp.einsum('bhgqc,bchd->bqhgd', p_c.astype(vc.dtype), vc)
        imp = jnp.einsum('bhgqc,cj->bhqj', p_c, overlap)
        cur = t // SEL_BLOCK
        j = jnp.arange(n_sel)[None, :]
        forced = (j == 0) | (j == cur[:, None]) | (j == cur[:, None] - 1)
        valid_blk = sel_start[None, :] <= t[:, None]
        imp = jnp.where(forced & valid_blk, FORCE_SCORE, jnp.where(valid_blk, imp, -1.0))
        top_val, top_idx = lax.top_k(imp, n_top)
        ks_g = ks_blocks[bi, hi, top_idx].reshape(B, NSA_KV_HEADS, Q_BLOCK, n_top * SEL_BLOCK, NSA_HEAD_DIM)
        vs_g = vs_blocks[bi, hi, top_idx].reshape(B, NSA_KV_HEADS, Q_BLOCK, n_top * SEL_BLOCK, NSA_HEAD_DIM)
        kpos = (top_idx[..., None] * SEL_BLOCK + blk_pos).reshape(B, NSA_KV_HEADS, Q_BLOCK, n_top * SEL_BLOCK)
        m_s = jnp.repeat(top_val >= 0, SEL_BLOCK, axis=-1) & (kpos <= t[None, None, :, None])
        s_s = jnp.einsum('bqhgd,bhqkd->bhgqk', qr, ks_g) * scale
        p_s = masked_softmax(s_s, m_s[:, :, None])
        o_s = jnp.einsum('bhgqk,bhqkd->bqhgd', p_s.astype(vs_g.dtype), vs_g)
        kw = lax.dynamic_slice_in_dim(kw_pad, blk * Q_BLOCK, Q_BLOCK + WINDOW, axis=1)
        vw = lax.dynamic_slice_in_dim(vw_pad, blk * Q_BLOCK, Q_BLOCK + WINDOW, axis=1)
        kpos_w = blk * Q_BLOCK - WINDOW + jnp.arange(Q_BLOCK + WINDOW)
        m_w = ((kpos_w[None, :] <= t[:, None]) & (kpos_w[None, :] > t[:, None] - WINDOW)
               & (kpos_w[None, :] >= 0))
        s_w = jnp.einsum('bqhgd,bkhd->bhgqk', qr, kw) * scale
        p_w = masked_softmax(s_w, m_w)
        o_w = jnp.einsum('bhgqk,bkhd->bqhgd', p_w.astype(vw.dtype), vw)
        g = g.reshape(B, Q_BLOCK, N_BRANCH, NSA_KV_HEADS, NSA_GROUP)[..., None]
        o = g[:, :, 0] * o_c + g[:, :, 1] * o_s + g[:, :, 2] * o_w
        return o.reshape(B, Q_BLOCK, NSA_Q_WIDTH).astype(h.dtype)

    out = lax.map(attend, (jnp.arange(nb), blockify(q), blockify(q_rope), blockify(gates)))
    return out.swapaxes(0, 1).reshape(B, S, NSA_Q_WIDTH) @ w_out

def first_inputs(seed: int = 0) -> dict:
    key = jax.random.key(seed)
    ks = jax.random.split(key, 24)
    D = D_MODEL

    def nrm(k, shape, scale):
        return jax.random.normal(k, shape, jnp.float32) * scale

    def gain(k, shape):
        return 1.0 + nrm(k, shape, 0.02)

    return {
        'x': nrm(ks[0], (BATCH, SEQ, D), 1.0),
        'c': nrm(ks[1], (BATCH, D), 1.0),
        'ada_w': nrm(ks[2], (2 * DEPTH, D, 3 * D), 0.5 * D ** -0.5),
        'ada_b': nrm(ks[3], (2 * DEPTH, 3 * D), 0.02),
        'norm_mix': gain(ks[4], (DEPTH, D)),
        'norm_ffn': gain(ks[5], (DEPTH, D)),
        'hgrn_w_in': nrm(ks[6], (N_A_LAYERS, D, 2 * HGRN_D_KEY + 2 * HGRN_D_VAL), D ** -0.5),
        'hgrn_lower_bounds': nrm(ks[7], (N_A_LAYERS, HGRN_D_KEY), 0.5),
        'hgrn_out_norm': gain(ks[8], (N_A_LAYERS, HGRN_DV)),
        'hgrn_w_out': nrm(ks[9], (N_A_LAYERS, HGRN_D_VAL, D), HGRN_D_VAL ** -0.5),
        'kv_ada_w': nrm(ks[10], (D, 2 * D), 0.5 * D ** -0.5),
        'kv_ada_b': nrm(ks[11], (2 * D,), 0.02),
        'kv_norm': gain(ks[12], (D,)),
        'nsa_w_kv': nrm(ks[13], (D, 2 * N_BRANCH * NSA_KV_HEADS * NSA_HEAD_DIM), D ** -0.5),
        'nsa_k_norm': gain(ks[14], (N_BRANCH, NSA_HEAD_DIM)),
        'cmp_pos': nrm(ks[15], (2, CMP_BLOCK, NSA_HEAD_DIM), 0.1),
        'cmp_w1': nrm(ks[16], (2, CMP_BLOCK * NSA_HEAD_DIM, CMP_HIDDEN), (CMP_BLOCK * NSA_HEAD_DIM) ** -0.5),
        'cmp_w2': nrm(ks[17], (2, CMP_HIDDEN, NSA_HEAD_DIM), CMP_HIDDEN ** -0.5),
        'nsa_w_q': nrm(ks[18], (N_B_LAYERS, D, NSA_Q_WIDTH + N_BRANCH * NSA_HEADS), D ** -0.5),
        'nsa_q_norm': gain(ks[19], (N_B_LAYERS, NSA_HEAD_DIM)),
        'nsa_w_out': nrm(ks[20], (N_B_LAYERS, NSA_Q_WIDTH, D), NSA_Q_WIDTH ** -0.5),
        'ffn_w_in': nrm(ks[21], (DEPTH, D, 2 * FFN_HIDDEN), D ** -0.5),
        'ffn_w_out': nrm(ks[22], (DEPTH, FFN_HIDDEN, D), FFN_HIDDEN ** -0.5),
    }

def first_block(x, c, ada_w, ada_b, norm_mix, norm_ffn, hgrn_w_in, hgrn_lower_bounds, hgrn_out_norm,
              hgrn_w_out, kv_ada_w, kv_ada_b, kv_norm, nsa_w_kv, nsa_k_norm, cmp_pos, cmp_w1, cmp_w2,
              nsa_w_q, nsa_q_norm, nsa_w_out, ffn_w_in, ffn_w_out):
    B, S, _ = x.shape
    cos, sin = rope_tables(S, NSA_HEAD_DIM)
    c_act = jax.nn.silu(c)
    mods = jnp.einsum('bd,lde->lbe', c_act, ada_w) + ada_b[:, None, :]
    lb = jax.nn.softmax(hgrn_lower_bounds.astype(jnp.float32), axis=0)
    lb = jnp.cumsum(lb, axis=0) - lb[0]
    shared = None
    for layer in range(DEPTH):
        shift, scale, gate = jnp.split(mods[2 * layer], 3, axis=-1)
        h = modulate(x, norm_mix[layer], shift, scale)
        if layer < N_A_LAYERS:
            y = hgrn2_mixer(h, hgrn_w_in[layer], lb[layer], hgrn_out_norm[layer], hgrn_w_out[layer], layer == 0)
        else:
            if layer == N_A_LAYERS:
                kv_shift, kv_scale = jnp.split(c_act @ kv_ada_w + kv_ada_b, 2, axis=-1)
                shared = nsa_shared_kv(modulate(x, kv_norm, kv_shift, kv_scale), nsa_w_kv, nsa_k_norm,
                                       cmp_pos, cmp_w1, cmp_w2, cos, sin)
            bl = layer - N_A_LAYERS
            y = nsa_mixer(h, nsa_w_q[bl], nsa_q_norm[bl], nsa_w_out[bl], shared, cos, sin)
        x = x + gate[:, None, :] * y
        shift, scale, gate = jnp.split(mods[2 * layer + 1], 3, axis=-1)
        h = modulate(x, norm_ffn[layer], shift, scale)
        x = x + gate[:, None, :] * swiglu(h, ffn_w_in[layer], ffn_w_out[layer])
    return x


N_MIXERS = 2
N_HEADS = 8
HEAD_DIM = D_MODEL // (2 * N_HEADS)
V_HEAD_DIM = 2 * HEAD_DIM
SSM_GROUP = 16
N_GROUPS = D_MODEL // SSM_GROUP
SSM_STATE = 64
DT_MIN = 1e-3
DT_MAX = 1e-1
D_FF = 4 * D_MODEL
RMS_EPS = 1e-6
N_ATTN_LAYERS = (DEPTH + 1) // 2
N_SSM_LAYERS = DEPTH // 2


def rms_norm_2(x, gain):
    xf = x.astype(jnp.float32)
    y = xf * lax.rsqrt(jnp.mean(xf * xf, axis=-1, keepdims=True) + RMS_EPS)
    return (y * gain.astype(jnp.float32)).astype(x.dtype)

def rope_tables_2(seq):
    pos = jnp.arange(seq, dtype=jnp.float32)
    inv_freq = ROPE_THETA ** (-jnp.arange(0, HEAD_DIM, 2, dtype=jnp.float32) / HEAD_DIM)
    ang = pos[:, None] * inv_freq[None, :]
    return jnp.cos(ang), jnp.sin(ang)

def apply_rope_2(t, cos, sin):
    tf = t.astype(jnp.float32)
    t1, t2 = jnp.split(tf, 2, axis=-1)
    c = cos[None, :, None, None, :]
    s = sin[None, :, None, None, :]
    out = jnp.concatenate([t1 * c - t2 * s, t2 * c + t1 * s], axis=-1)
    return out.astype(t.dtype)

def lambda_init(layer_idx):
    return 0.8 - 0.6 * math.exp(-0.3 * layer_idx)

def diff_attention(u, w_qkv, q_gain, k_gain, lam_vecs, subln_gain, w_o, lam_init, cos, sin):
    b, s, _ = u.shape
    qkv = u @ w_qkv
    q, k, v = jnp.split(qkv, 3, axis=-1)
    q = q.reshape(b, s, N_HEADS, 2, HEAD_DIM)
    k = k.reshape(b, s, N_HEADS, 2, HEAD_DIM)
    v = v.reshape(b, s, N_HEADS, V_HEAD_DIM)
    q = apply_rope_2(rms_norm_2(q, q_gain), cos, sin) * (HEAD_DIM ** -0.5)
    k = apply_rope_2(rms_norm_2(k, k_gain), cos, sin)
    lv = lam_vecs.astype(jnp.float32)
    lam = jnp.exp(jnp.sum(lv[0] * lv[1])) - jnp.exp(jnp.sum(lv[2] * lv[3])) + lam_init
    n_blocks = s // Q_BLOCK
    qb = q.reshape(b, n_blocks, Q_BLOCK, N_HEADS, 2, HEAD_DIM).transpose(1, 0, 2, 3, 4, 5)

    def block(q_blk):
        scores = jnp.einsum('bqhcd,bkhcd->bhcqk', q_blk, k,
                            preferred_element_type=jnp.float32)
        p = jax.nn.softmax(scores, axis=-1)
        attn = (p[:, :, 0] - lam * p[:, :, 1]).astype(v.dtype)
        return jnp.einsum('bhqk,bkhe->bqhe', attn, v)

    o = lax.map(block, qb)
    o = o.transpose(1, 0, 2, 3, 4).reshape(b, s, N_HEADS, V_HEAD_DIM)
    o = rms_norm_2(o, subln_gain) * (1.0 - lam_init)
    return o.reshape(b, s, D_MODEL) @ w_o

def _ssm_combine(e1, e2):
    a1, h1 = e1
    a2, h2 = e2
    return a1 * a2, a2 * h1 + h2

def s5_layer(u, a_re, a_im, log_dt, b_re, b_im, c_re, c_im, d_skip, w_glu):
    b, s, _ = u.shape
    f32 = jnp.float32
    lam = lax.complex(a_re.astype(f32), a_im.astype(f32))
    dt = jnp.exp(log_dt.astype(f32))[..., None]
    a_bar = jnp.exp(lam * dt)
    b_mat = lax.complex(b_re.astype(f32), b_im.astype(f32))
    b_bar = ((a_bar - 1.0) / lam)[..., None] * b_mat
    c_mat = lax.complex(c_re.astype(f32), c_im.astype(f32))
    ug = u.astype(f32).reshape(b, s, N_GROUPS, SSM_GROUP)

    def scan_dir(u_row, r, reverse):
        bu = jnp.einsum('sgh,gph->sgp', u_row.astype(jnp.complex64), b_bar[r])
        a = jnp.broadcast_to(a_bar[r], bu.shape)
        _, states = lax.associative_scan(_ssm_combine, (a, bu), reverse=reverse, axis=0)
        return jnp.einsum('sgp,ghp->sgh', states, c_mat[r]).real

    def row(u_row):
        return scan_dir(u_row, 0, False) + scan_dir(u_row, 1, True)

    y = lax.map(row, ug)
    y = y.reshape(b, s, D_MODEL) + d_skip.astype(f32) * u.astype(f32)
    g = jax.nn.gelu(y).astype(u.dtype)
    val, gate = jnp.split(g @ w_glu, 2, axis=-1)
    return val * jax.nn.sigmoid(gate)

def squared_relu_mlp(u, w_up, w_down):
    return jnp.square(jax.nn.relu(u @ w_up)) @ w_down

def second_inputs(seed: int = 0) -> dict:
    key = jax.random.key(seed)
    ks = jax.random.split(key, 24)
    f32 = jnp.float32
    D, NA, NS = D_MODEL, N_ATTN_LAYERS, N_SSM_LAYERS
    G, P, HG = N_GROUPS, SSM_STATE, SSM_GROUP
    nrm = lambda k, shape, scale: jax.random.normal(k, shape, f32) * scale
    gain = lambda k, shape: 1.0 + 0.02 * jax.random.normal(k, shape, f32)
    x = jax.random.normal(ks[0], (BATCH, SEQ, D), f32)
    a_re = -0.5 * jnp.exp(0.02 * jax.random.normal(ks[9], (NS, 2, G, P), f32))
    a_im = (math.pi * jnp.arange(P, dtype=f32))[None, None, None, :] + \
        0.01 * jax.random.normal(ks[10], (NS, 2, G, P), f32)
    log_dt = jax.random.uniform(ks[11], (NS, 2, G), f32,
                                minval=math.log(DT_MIN), maxval=math.log(DT_MAX))
    return {
        "x": x,
        "norm_mix": gain(ks[1], (DEPTH, D)),
        "norm_ffn": gain(ks[2], (DEPTH, D)),
        "attn_w_qkv": nrm(ks[3], (NA, D, 3 * D), D ** -0.5),
        "attn_q_gain": gain(ks[4], (NA, HEAD_DIM)),
        "attn_k_gain": gain(ks[5], (NA, HEAD_DIM)),
        "attn_lambda": nrm(ks[6], (NA, 4, HEAD_DIM), 0.1),
        "attn_subln": gain(ks[7], (NA, V_HEAD_DIM)),
        "attn_w_o": nrm(ks[8], (NA, D, D), D ** -0.5),
        "ssm_a_re": a_re,
        "ssm_a_im": a_im,
        "ssm_log_dt": log_dt,
        "ssm_b_re": nrm(ks[12], (NS, 2, G, P, HG), (2 * HG) ** -0.5),
        "ssm_b_im": nrm(ks[13], (NS, 2, G, P, HG), (2 * HG) ** -0.5),
        "ssm_c_re": nrm(ks[14], (NS, 2, G, HG, P), P ** -0.5),
        "ssm_c_im": nrm(ks[15], (NS, 2, G, HG, P), P ** -0.5),
        "ssm_d": nrm(ks[16], (NS, D), 1.0),
        "ssm_w_glu": nrm(ks[17], (NS, D, 2 * D), D ** -0.5),
        "ffn_w_up": nrm(ks[18], (DEPTH, D, D_FF), D ** -0.5),
        "ffn_w_down": nrm(ks[19], (DEPTH, D_FF, D), D_FF ** -0.5),
    }

def second_block(x, norm_mix, norm_ffn, attn_w_qkv, attn_q_gain, attn_k_gain, attn_lambda,
              attn_subln, attn_w_o, ssm_a_re, ssm_a_im, ssm_log_dt, ssm_b_re, ssm_b_im,
              ssm_c_re, ssm_c_im, ssm_d, ssm_w_glu, ffn_w_up, ffn_w_down):
    cos, sin = rope_tables_2(x.shape[1])
    h = x
    for i in range(DEPTH):
        u = rms_norm_2(h, norm_mix[i])
        j = i // N_MIXERS
        if i % N_MIXERS == 0:
            mix = diff_attention(u, attn_w_qkv[j], attn_q_gain[j], attn_k_gain[j],
                                 attn_lambda[j], attn_subln[j], attn_w_o[j],
                                 lambda_init(i), cos, sin)
        else:
            mix = s5_layer(u, ssm_a_re[j], ssm_a_im[j], ssm_log_dt[j], ssm_b_re[j],
                           ssm_b_im[j], ssm_c_re[j], ssm_c_im[j], ssm_d[j], ssm_w_glu[j])
        h = h + mix.astype(h.dtype)
        h = h + squared_relu_mlp(rms_norm_2(h, norm_ffn[i]), ffn_w_up[i], ffn_w_down[i]).astype(h.dtype)
    return h


def setup_inputs(seed=0):
    out = dict(first_inputs(seed))
    for name, value in second_inputs(seed + 1).items():
        if name != "x":
            out[name + "_2"] = value
    return out


def reference(
    x, c, ada_w, ada_b, norm_mix, norm_ffn, hgrn_w_in, hgrn_lower_bounds, hgrn_out_norm,
    hgrn_w_out, kv_ada_w, kv_ada_b, kv_norm, nsa_w_kv, nsa_k_norm, cmp_pos, cmp_w1, cmp_w2,
    nsa_w_q, nsa_q_norm, nsa_w_out, ffn_w_in, ffn_w_out, norm_mix_2, norm_ffn_2, attn_w_qkv_2,
    attn_q_gain_2, attn_k_gain_2, attn_lambda_2, attn_subln_2, attn_w_o_2, ssm_a_re_2,
    ssm_a_im_2, ssm_log_dt_2, ssm_b_re_2, ssm_b_im_2, ssm_c_re_2, ssm_c_im_2, ssm_d_2,
    ssm_w_glu_2, ffn_w_up_2, ffn_w_down_2,
):
    x = first_block(
        x, c, ada_w, ada_b, norm_mix, norm_ffn, hgrn_w_in, hgrn_lower_bounds, hgrn_out_norm,
        hgrn_w_out, kv_ada_w, kv_ada_b, kv_norm, nsa_w_kv, nsa_k_norm, cmp_pos, cmp_w1, cmp_w2,
        nsa_w_q, nsa_q_norm, nsa_w_out, ffn_w_in, ffn_w_out,
    )
    return second_block(
        x, norm_mix_2, norm_ffn_2, attn_w_qkv_2, attn_q_gain_2, attn_k_gain_2, attn_lambda_2,
        attn_subln_2, attn_w_o_2, ssm_a_re_2, ssm_a_im_2, ssm_log_dt_2, ssm_b_re_2, ssm_b_im_2,
        ssm_c_re_2, ssm_c_im_2, ssm_d_2, ssm_w_glu_2, ffn_w_up_2, ffn_w_down_2,
    )


_drawn_inputs = setup_inputs


def setup_inputs(seed=0):
    import zlib

    import numpy as np

    out = dict(_drawn_inputs(seed))
    spreads = {}
    factors = {'norm_mix': 8.0,
     'norm_ffn': 5.755,
     'hgrn_out_norm': 8.0,
     'kv_norm': 8.0,
     'nsa_k_norm': 8.0,
     'nsa_q_norm': 8.0,
     'norm_mix_2': 3.043,
     'norm_ffn_2': 11.069,
     'attn_q_gain_2': 6.32,
     'attn_k_gain_2': 4.954,
     'attn_subln_2': 110.816,
     'ssm_a_re_2': 200.0,
     'cmp_pos': 6.306,
     'attn_lambda_2': 3.164,
     'ssm_a_im_2': 64.0,
     'ssm_log_dt_2': 64.0,
     'ssm_b_re_2': 64.0,
     'ssm_b_im_2': 64.0,
     'ssm_c_re_2': 64.0,
     'ssm_c_im_2': 64.0,
     'ssm_d_2': 6.833,
     'ssm_w_glu_2': 5.863}
    for name, (base, spread) in spreads.items():
        noise = np.random.default_rng([zlib.crc32(name.encode()), seed]).standard_normal(out[name].shape)
        drawn = base * np.exp(spread * noise) if base else spread * noise
        out[name] = __import__('jax').numpy.asarray(drawn.astype(out[name].dtype))
    for name, factor in factors.items():
        out[name] = (out[name] * factor).astype(out[name].dtype)
    return out
```

```python
from contextlib import ExitStack

import numpy as np

import concourse.bass as bass
from concourse import mybir

F32 = mybir.dt.float32
F32R = mybir.dt.float32r
ACT = mybir.ActivationFunctionType
ALU = mybir.AluOpType
AX = mybir.AxisListType

P = 128
D = 1024
T = 512
KT = D // P
TT = T // P
FF1 = 2816
FF2 = 4096
NH = 8
CH = 16
NCH = T // CH
KVH = 4
EPS = 1e-6
NEG = -1e30
SLOT = 2048
GH = 16
NG5 = D // GH
L8 = 8
NC8 = T // L8
NB5 = NG5 // 4
PITCH = P + CH
HEAD_SPAN = P * PITCH + PITCH

ROWS = {}
_n = 0
for _name, _k in [("ada_b", 96), ("kv_ada_b", 16), ("c", 8)]:
    ROWS[_name] = _n
    _n += _k
NROW_A = _n
_n = 0
for _name, _k in [("norm_mix", 16), ("norm_ffn", 16), ("kv_norm", 8), ("norm_mix_2", 16),
                  ("norm_ffn_2", 16), ("ssm_d_2", 8), ("hgrn_out_norm", 1), ("attn_subln_2", 1),
                  ("cmp_pos", 32), ("gains", 6)]:
    ROWS[_name] = _n
    _n += _k
NROW_B = _n


class Segment:

    def __init__(self, name, n, source, act, dve, width=256, ktiles=8, ada=None):
        self.name, self.n, self.source = name, n, source
        self.ada = ada
        self.act, self.dve, self.units = act, dve, act + dve
        self.width, self.ktiles = width, ktiles


def build(nc, a, out, upto=99):
    ctx = ExitStack()
    with ctx:
        def sb(name, shape, dt=F32, where=ctx):
            return where.enter_context(nc.sbuf_tensor(name, shape, dt))

        def sem(name):
            return ctx.enter_context(nc.semaphore(name))

        xT = sb("xT", [P, KT, T])
        with ExitStack() as over:
            hh = sb("hh", [P, KT, T], F32R, over)
            hl = sb("hl", [P, KT, T], F32R, over)
        h_area = sb("h_area", [P, 2 * KT * T])
        raw = sb("raw", [P, 2, SLOT])
        whi = sb("whi", [P, 2, SLOT], F32R)
        wlo = sb("wlo", [P, 2, SLOT], F32R)
        ident = sb("ident", [P, P])
        ones = sb("ones", [P, P])
        cols_a = sb("cols_a", [P, NROW_A])
        cols_b = sb("cols_b", [P, NROW_B])
        mods = sb("mods", [P, 112])
        cact = sb("cact", [P, KT])
        ada_ring = sb("ada_ring", [P, 2, D])
        ada_acc = sb("ada_acc", [P, 2, P])
        gains_a = sb("gains_a", [P, 7, KT])
        zero_col = sb("zero_col", [P, 1])
        eps_col = sb("eps_col", [P, 1])
        rstd = sb("rstd", [P, T])
        sq = sb("sq", [P, 2, T])
        xn = sb("xn", [P, 2, T])

        ps = ctx.enter_context(nc.psum_tensor("ps", [P, 8, T], F32))

        def scope(*tensors):
            with ExitStack() as s:
                return [sb(n, shape, dt, s) for n, shape, dt in tensors]

        xin, vec_a, vec_b, ada_first = scope(
            ("xin", [P, TT, D], F32), ("vec_a", [P, P], F32), ("vec_b", [P, P], F32),
            ("ada_first", [P, 6, SLOT], F32))
        qT, fT, kT, vS, scr1, scr2, state, evenodd = scope(
            ("qT", [P, NH, T], F32), ("fT", [P, NH, T], F32), ("kT", [P, NH, T], F32),
            ("vS", [P, TT, D], F32), ("scr1", [P, NH * T], F32),
            ("scr2", [P, NH * T], F32), ("state", [P, 2, NH, P], F32), ("evenodd", [P, 2], F32))
        gT = scr1[:, :].rearrange("p (h t) -> p h t", h=NH)
        decay = sq[:, 1, 0:NH * NCH].rearrange("p (h c) -> p h c", h=NH)
        sel = sq[:, 1, NH * NCH:NH * NCH + 2 * P - 1]
        band, bandT = sq[:, 0, :], rstd[:, :].rearrange("p (t n) -> p t n", t=TT)
        hid_h, hid_l, act_t, hid_f = scope(
            ("hid_h", [P, 16, T], F32R), ("hid_l", [P, 16, T], F32R),
            ("act_t", [P, 2, T], F32), ("hid_f", [P, 2, T], F32))

        def carve(area):
            place = [0]

            def take(n, at=None):
                at = place[0] if at is None else at
                place[0] = max(place[0], at + n)
                return area[:, at:at + n]
            return take

        nsa_area, gwh, gwl = scope(("nsa_area", [P, 25344], F32), ("gwh", [P, KT * 48], F32R),
                                   ("gwl", [P, KT * 48], F32R))
        take = carve(nsa_area)
        rope_c = take(1024 + 256)
        cosT, sinT, rotm, blk64 = rope_c[:, 0:T], rope_c[:, T:2 * T], rope_c[:, 1024:1152], rope_c[:, 1152:1280]
        nsa_c = take(4 * P + P + 4 * 32 + 4)
        dup = [nsa_c[:, i * P:(i + 1) * P] for i in range(2)]
        rotdup = [nsa_c[:, (2 + i) * P:(3 + i) * P] for i in range(2)]
        causal, cmpmask, valid = nsa_c[:, 512:640], nsa_c[:, 640:768], nsa_c[:, 768:772]
        v_sel, v_win = (take(TT * 256).rearrange("p (t n) -> p t n", t=TT) for _ in range(2))
        k_sel, k_win = (take(KVH * T).rearrange("p (g t) -> p g t", g=KVH) for _ in range(2))
        nq = take(KT * T).rearrange("p (k t) -> p k t", k=KT)
        at = 12292
        kvc = take(4 * T, at).rearrange("p (k t) -> p k t", k=4)
        nqr = take(KT * T, at).rearrange("p (k t) -> p k t", k=KT)
        at += KT * T
        w1v = take(16 * 256, at).rearrange("p (m n) -> p m n", m=16)
        no = take(TT * D, at).rearrange("p (t n) -> p t n", t=TT)
        at += TT * D
        ksr = take(2 * T, at).rearrange("p (k t) -> p k t", k=2)
        kwr = take(2 * T, at + 2 * T).rearrange("p (k t) -> p k t", k=2)
        gw = take(KT * 48, at + 4 * T)
        pbuf = take(4 * T, at).rearrange("p (k t) -> p k t", k=4)
        ptbuf = take(2 * T, at + 4 * T).rearrange("p (k t) -> p k t", k=2)
        at += 6 * T
        rope_t = ptbuf
        vblk = take(4 * 256, at).rearrange("p (g n) -> p g n", g=4)
        kcT = take(4 * 32).rearrange("p (g n) -> p g n", g=4)
        gates = take(TT * 48).rearrange("p (t n) -> p t n", t=TT)
        small, otmp = take(160), take(256)
        hidc = take(4 * 124, 14340).rearrange("p (k n) -> p k n", k=4)
        w2 = take(256 + 128, 14340 + 496)
        dq = take(KT * T, 1280).rearrange("p (k t) -> p k t", k=KT)
        dk = take(KT * T, 1280 + 4096).rearrange("p (k t) -> p k t", k=KT)
        dv = take(TT * D, 1280 + 2 * 4096).rearrange("p (t n) -> p t n", t=TT)
        do = take(TT * D, 1280 + 3 * 4096).rearrange("p (t n) -> p t n", t=TT)
        dp = take(4 * T, 17664).rearrange("p (buf c n) -> p buf c n", buf=2, c=2)
        dc = take(2 * T, 17664 + 2048).rearrange("p (buf n) -> p buf n", buf=2)
        dpt = take(2 * T, 17664 + 3072).rearrange("p (buf n) -> p buf n", buf=2)
        d_small = take(128, 23556)
        lam_vec, lam_tmp, d_sq = take(256, 23684), take(128, 23940), take(P, 24068)
        w1k = h_area[:, 4096:8192].rearrange("p (m n) -> p m n", m=16)
        gk = h_area[:, 0:2048].rearrange("p (g t) -> p g t", g=4)
        gv = h_area[:, 2048:4096].rearrange("p (g t) -> p g t", g=4)

        (s5_area,) = scope(("s5_area", [P, 26560], F32))
        take = carve(s5_area)
        u_tok = take(8192)[0:NC8, :].rearrange("c (g t h) -> c g t h", t=L8, h=GH)
        y_tok = s5_area[0:NC8, 0:8192].rearrange("c (t d) -> c t d", t=L8)
        a_raw = s5_area[0:64, 0:256].rearrange("g (n m) -> g n m", n=2)
        log_dt = s5_area[:, 256:320]
        H = take(8192).rearrange("p (ri g s) -> p ri g s", ri=2, g=NG5)
        bc_raw = s5_area[0:64, 8192:16384].rearrange("g (n m) -> g n m", n=4)
        b_bar = take(2048).rearrange("p (ri g h) -> p ri g h", ri=2, g=NG5)
        c_mat = take(2048).rearrange("p (ri g h) -> p ri g h", ri=2, g=NG5)
        pw = take(2 * 9 * NG5).rearrange("p (ri k g) -> p ri k g", ri=2, k=9)
        pw_in = take(1024).rearrange("p (ri g t) -> p ri g t", ri=2, g=NG5)
        pw_out = take(1024).rearrange("p (ri g t) -> p ri g t", ri=2, g=NG5)
        at = 23680
        par5 = [take(64, at + 64 * i) for i in range(15)]
        bb_tmp = take(1024, 24640)
        tmp_in = take(2048, at).rearrange("p (buf n) -> p buf n", buf=2)
        g_sb = take(960, at)[0:GH, :].rearrange("p (g n) -> p g n", g=4)
        ub = take(512, at + 960).rearrange("p (buf g c) -> p buf g c", buf=2, g=4)
        bb = take(256, at + 1472).rearrange("p (buf ri g h) -> p buf ri g h", buf=2, ri=2, g=4)
        tmp_out = take(1024, at + 1728)
        scan_t = take(256, at + 1728).rearrange("p (buf ri g) -> p buf ri g", buf=2, ri=2)
        a8i = take(2 * NG5).rearrange("p (ri g) -> p ri g", ri=2)
        uT = h_area[:, 0:4096].rearrange("p (k t) -> p k t", k=KT)
        u_all = h_area[:, 4096:8192].rearrange("p (g c) -> p g c", g=NG5)
        sb_ = h_area[:, 0:2048].rearrange("p (buf ri g n) -> p buf ri g n", buf=2, ri=2, g=4)
        sbt = h_area[:, 2048:4096].rearrange("p (buf ri g n) -> p buf ri g n", buf=2, ri=2, g=4)
        cp = sb_
        toep = h_area[:, 2048:3072].rearrange("p (buf g n) -> p buf g n", buf=2, g=4)
        hb = h_area[:, 3072:4096].rearrange("p (buf ri g c) -> p buf ri g c", buf=2, ri=2, g=4)

        w_dma = [sem("w_dma_even"), sem("w_dma_odd")]
        w_hi = sem("w_hi")
        w_lo = sem("w_lo")
        mm = sem("mm")
        ev_a = sem("ev_a")
        ev_v = sem("ev_v")
        const_in = sem("const_in")
        x_in = sem("x_in")
        sq_rdy, ssq_rdy, rstd_rdy = sem("sq_rdy"), sem("ssq_rdy"), sem("rstd_rdy")
        xn_rdy, hh_rdy, hl_rdy = sem("xn_rdy"), sem("hh_rdy"), sem("hl_rdy")
        a_link, v_link, pool_set = sem("a_link"), sem("v_link"), sem("pool_set")
        cols_rdy, cols_ps = sem("cols_rdy"), sem("cols_ps")
        cact_rdy, mods_rdy = sem("cact_rdy"), sem("mods_rdy")
        ada0_in = [sem(f"ada0_in{i}") for i in range(6)]
        ada0_used = sem("ada0_used")
        ada_in = [sem("ada_in_even"), sem("ada_in_odd")]
        ada_rdy = sem("ada_rdy")
        ada_used = sem("ada_used")
        ada_step = sem("ada_step")
        ada_mm = sem("ada_mm")
        ada0_sum_v, ada0_sum_g = sem("ada0_sum_v"), sem("ada0_sum_g")
        out_rdy, stored, out_ps = sem("out_rdy"), sem("stored"), sem("out_ps")

        def cols_of(w, first, step=256):
            v = w.rearrange("(k p) n -> p k n", p=P)
            return lambda b, at: v[:, :, bass.ds(at(b * step + first), step)]

        def pair_of(w, first=0):
            v = w.rearrange("(k p) (j n) -> p j k n", p=P, j=2)
            return lambda b, at: v[:, :, :, bass.ds(at(b * P + first), P)]

        def rows_of(w, row0, ktiles):
            v = w[row0:row0 + ktiles * P, :].rearrange("(k p) n -> p k n", p=P)
            return lambda b, at: v[:, :, bass.ds(at(b * P), P)]

        w_in = a["hgrn_w_in"][0]
        segs = []

        def add(*args, **kw):
            segs.append(Segment(*args, **kw))

        def ada_part(layer, first, per):
            return a["ada_w"][layer], first, 24 * layer + first, per

        def add_ffn1(layer):
            for half in range(2):
                ada_in = (ada_part(2, 0, 1), ada_part(3, 0, 2))[half] if layer == 0 else None
                ada = ada_part(2, (11, 16)[half], 1) if layer == 0 else None
                add(f"ffn{layer}_in{half}", 11, pair_of(a["ffn_w_in"][layer], half * 11 * P), 1, 1, P, ada=ada_in)
                add(f"ffn{layer}_out{half}", 8, rows_of(a["ffn_w_out"][layer], half * 11 * P, 11), 0, 1, P, 11, ada=ada)

        def add_mlp(layer):
            for half in range(2):
                add(f"mlp{layer}_in{half}", 8, cols_of(a["ffn_w_up_2"][layer], half * 16 * P), 2, 0)
                add(f"mlp{layer}_out{half}", 8, rows_of(a["ffn_w_down_2"][layer], half * 16 * P, 16), 0, 1, P, 16)

        if upto >= 2:
            add("h_q", 4, cols_of(w_in, 0), 2, 0, ada=ada_part(1, 0, 2))
            add("h_f", 4, cols_of(w_in, D), 2, 0, ada=ada_part(1, 8, 2))
            add("h_v", 4, cols_of(w_in, 2 * D), 0, 2, ada=ada_part(1, 16, 2))
        if upto >= 3:
            add("h_g", 4, cols_of(w_in, 3 * D), 2, 0, ada=(a["kv_ada_w"], 0, 96, 2))
        if upto >= 4:
            add("h_out", 4, cols_of(a["hgrn_w_out"][0], 0), 0, 2, ada=(a["kv_ada_w"], 8, 104, 2))
        if upto >= 5:
            add_ffn1(0)
        if upto >= 6:
            w_kv = a["nsa_w_kv"]
            add("n_kvc", 2, cols_of(w_kv, 0), 2, 0, ada=ada_part(3, 22, 1))
            add("n_ks", 1, cols_of(w_kv, 512), 2, 0)
            add("n_vs", 1, cols_of(w_kv, 768), 0, 2)
            add("n_kw", 1, cols_of(w_kv, 1024), 2, 0)
            add("n_vw", 1, cols_of(w_kv, 1280), 0, 2)
            add("n_q", 4, cols_of(a["nsa_w_q"][0], 0), 2, 0)
        if upto >= 7:
            add("n_out", 4, cols_of(a["nsa_w_out"][0], 0), 0, 2)
        if upto >= 8:
            add_ffn1(1)
        if upto >= 9:
            w_qkv = a["attn_w_qkv_2"][0]
            add("d_q", 4, cols_of(w_qkv, 0), 2, 0)
            add("d_k", 4, cols_of(w_qkv, D), 2, 0)
            add("d_v", 4, cols_of(w_qkv, 2 * D), 0, 2)
            add("d_out", 4, cols_of(a["attn_w_o_2"][0], 0), 0, 2)
        if upto >= 10:
            add_mlp(0)
        if upto >= 11:
            add("s_glu", 8, pair_of(a["ssm_w_glu_2"][0]), 1, 1, P)
        if upto >= 12:
            add_mlp(1)

        FIRST_UNITS = 8
        g0, mm0, ea0, ev0 = 0, FIRST_UNITS, 0, FIRST_UNITS
        for s in segs:
            s.g0, s.mm0, s.ea0, s.ev0 = g0, mm0, ea0, ev0
            g0, mm0 = g0 + s.n, mm0 + s.n * s.units
            ea0, ev0 = ea0 + s.n * s.act, ev0 + s.n * s.dve
        blocks = g0
        ada0 = 0
        for s in segs:
            s.ada0, s.ada_seg = ada0, sum(bool(x.ada) for x in segs[:segs.index(s)])
            ada0 += s.n * s.ada[3] if s.ada else 0
        seg = {s.name: s for s in segs}

        def after(s):
            return s.mm0 + s.n * s.units, s.ea0 + s.n * s.act, s.ev0 + s.n * s.dve

        norm_after = {"h_out": 1, "ffn0_out1": 2, "n_out": 3, "ffn1_out1": 4, "d_out": 5, "mlp0_out1": 6,
                      "s_glu": 7} if upto >= 12 else {}

        def each_block(eng, s, body, peel=False):
            pairs = s.n // 2
            first = 1 if s.g0 == 0 or peel else 0
            last = pairs - 1 if s.g0 + s.n == blocks and s.n % 2 == 0 else pairs
            if first:
                body(0, 0, True)
                body(1, 1, True)
            if last - first > 1:
                with eng.Fori(first, last) as i:
                    for u in range(2):
                        body(i * 2 + u, (s.g0 + u) % 2, True)
            elif last - first == 1:
                for u in range(2):
                    body(2 * first + u, (s.g0 + u) % 2, True)
            for b in range(2 * last, s.n):
                body(b, (s.g0 + b) % 2, s.g0 + b + 2 < blocks)

        def landed(s, b, par, ahead):
            return (b + (s.g0 + ahead - par)) * 8 + 16

        def convert_hi(act, s, b, par, ahead):
            act.wait_ge(w_dma[par], landed(s, b, par, ahead))
            if ahead == 2:
                act.wait_ge(mm, (b + 1) * s.units + s.mm0)
            nc.scalar.activation(whi[:, par, :], raw[:, par, :], ACT.Copy).then_inc(w_hi, 1)

        def convert_lo(dve, s, b, par, ahead):
            dve.wait_ge(w_hi, b + (s.g0 + ahead + 1))
            nc.vector.tensor_tensor(wlo[:, par, :], raw[:, par, :], whi[:, par, :].bitcast(F32),
                                    ALU.subtract).then_inc(w_lo, 1)

        def weight_products(pe, s, b, par, hi, lo, token_major=False, need=None):
            pe.wait_ge(w_lo, b + (s.g0 + 1))
            k = s.ktiles
            wh = whi[:, par, 0:k * s.width * (2 if s.width == P and k == 8 else 1)]
            wl = wlo[:, par, 0:k * s.width * (2 if s.width == P and k == 8 else 1)]
            if s.width == P and k == 8:
                wh = wh.rearrange("p (j k n) -> p j k n", j=2, k=k)
                wl = wl.rearrange("p (j k n) -> p j k n", j=2, k=k)
                tile = lambda w, kt, j: w[:, j, kt, :]
            else:
                wh = wh.rearrange("p (k n) -> p k n", k=k)
                wl = wl.rearrange("p (k n) -> p k n", k=k)
                tile = lambda w, kt, j: w[:, kt, j * P:(j + 1) * P]
            for ev, base, per in ((ev_a, s.ea0, s.act), (ev_v, s.ev0, s.dve)):
                if per and not (isinstance(b, int) and (b - 1) * per + base <= 0):
                    pe.wait_ge(ev, (b - 1) * per + base)
            for j in range(s.units):
                bank = 2 * par + j
                if token_major:
                    for half in range(2):
                        t0 = (2 * j + half) * P
                        for kt in range(k):
                            for n, (x, w) in enumerate(((hi, wh), (lo, wh), (hi, wl))):
                                m = nc.tensor.matmul(
                                    ps[:, bank, half * 256:half * 256 + 256], x[:, kt, t0:t0 + P],
                                    w[:, kt, :], start=(kt == 0 and n == 0), stop=(kt == k - 1 and n == 2))
                else:
                    for kt in range(k):
                        if need is not None and j == 0:
                            pe.wait_ge(hl_rdy, need + kt + 1)
                        for n, (x, w) in enumerate(((hi, wh), (lo, wh), (hi, wl))):
                            m = nc.tensor.matmul(ps[:, bank, :], tile(w, kt, j), x[:, kt, :],
                                                 start=(kt == 0 and n == 0), stop=(kt == k - 1 and n == 2))
                m.then_inc(mm, 1)

        def ada_slots(s, b, par):
            if s.ada:
                _, _, _, per = s.ada
                for i in range(per):
                    u = (par + s.g0) % 2
                    yield (s.ada0 + u * per + i) % 2, b * per + (s.ada0 + i), b * per + i

        def ada_products(pe, s, b, par):
            for slot, count, tile in ada_slots(s, b, par):
                pe.wait_ge(ada_used, count + 1)
                nc.tensor.matmul(ps[:, 5 + s.ada_seg % 2, bass.ds(tile + s.ada[2], 1)], ada_acc[:, slot, :],
                                 ones[:, 0:1], start=True, stop=True).then_inc(ada_mm, 1)

        def ada_sums(pool, s):
            def body(b, par, more):
                for slot, count, tile in ada_slots(s, b, par):
                    pool.wait_ge(ada_in[slot], (count - slot) * 8 + 16)
                    if not isinstance(count, int) or count >= 2:
                        pool.wait_ge(ada_mm, count - 1)
                    w = ada_ring[:, slot, :].rearrange("p (k n) -> p k n", k=KT)
                    nc.gpsimd.tensor_tensor(w, w, cact[:, :].unsqueeze(2).broadcast_to((P, KT, P)), ALU.mult
                                            ).then_inc(ada_step, 1)
                    pool.wait_ge(ada_step, count * 3 + 1)
                    nc.gpsimd.tensor_tensor(w[:, 0:4, :], w[:, 0:4, :], w[:, 4:8, :], ALU.add).then_inc(ada_step, 1)
                    pool.wait_ge(ada_step, count * 3 + 2)
                    nc.gpsimd.tensor_tensor(w[:, 0:2, :], w[:, 0:2, :], w[:, 2:4, :], ALU.add).then_inc(ada_step, 1)
                    pool.wait_ge(ada_step, count * 3 + 3)
                    nc.gpsimd.tensor_tensor(ada_acc[:, slot, :], w[:, 0, :], w[:, 1, :], ALU.add
                                            ).then_inc(ada_used, 1)
            if s.ada:
                each_block(pool, s, body)

        def ada_first_dve(dve):
            n = 0
            for m in DVE_FIRST:
                dve.wait_ge(ada0_in[m % 6], 16 * (m // 6 + 1))
                w = ada_first[:, m % 6, :].rearrange("p (k n) -> p k n", k=KT)
                nc.vector.tensor_scalar(w[:, 0, :], w[:, 0, :], cact[:, 0:1], None, ALU.mult).then_inc(ada0_sum_v, 1)
                for kt in range(1, KT):
                    dve.wait_ge(ada0_sum_v, n + kt)
                    nc.vector.scalar_tensor_tensor(out=w[:, 0, :], in0=w[:, kt, :], scalar=cact[:, kt:kt + 1],
                                                   in1=w[:, 0, :], op0=ALU.mult, op1=ALU.add).then_inc(ada0_sum_v, 1)
                n += KT

        def ada_first_pool(pool):
            n = 0
            for m in POOL_FIRST:
                pool.wait_ge(ada0_in[m % 6], 16 * (m // 6 + 1))
                w = ada_first[:, m % 6, :].rearrange("p (k n) -> p k n", k=KT)
                nc.gpsimd.tensor_tensor(w, w, cact[:, :].unsqueeze(2).broadcast_to((P, KT, 256)), ALU.mult
                                        ).then_inc(ada0_sum_g, 1)
                for half in (4, 2, 1):
                    n += 1
                    pool.wait_ge(ada0_sum_g, n)
                    nc.gpsimd.tensor_tensor(w[:, 0:half, :], w[:, 0:half, :], w[:, half:2 * half, :], ALU.add
                                            ).then_inc(ada0_sum_g, 1)
                n += 1

        DVE_FIRST, POOL_FIRST = [m for m in range(12) if m % 3 < 2], [m for m in range(12) if m % 3 == 2]

        def ada_bias(dve, s):
            if s.ada:
                n, at = s.n * s.ada[3], s.ada[2]
                dve.wait_ge(ada_mm, s.ada0 + n)
                nc.vector.tensor_tensor(mods[:, at:at + n], ps[:, 5 + s.ada_seg % 2, at:at + n],
                                        cols_a[:, at:at + n], ALU.add
                                        ).then_inc(ada_rdy, 1)

        def boundary(pe, s):
            if s.ea0:
                pe.wait_ge(ev_a, s.ea0)
            pe.wait_ge(ev_v, s.ev0)

        def mod_cols(which):
            if which == "kv":
                return gains_a[:, 6, :], mods[:, 96:104]
            layer = which
            return gains_a[:, layer, :], mods[:, 24 * layer:24 * layer + 8]


        band_dram = nc.dram_tensor("band_dram", [TT * NH, HEAD_SPAN], F32)
        band_rdy = sem("band_rdy")
        band_zero, band_out, band_in = sem("band_zero"), sem("band_out"), sem("band_in")
        prod_v, prod_g, lag_rdy, band_mm = sem("prod_v"), sem("prod_g"), sem("lag_rdy"), sem("band_mm")
        band_sb, bandT_ps, bandT_sb = sem("band_sb"), sem("bandT_ps"), sem("bandT_sb")
        q_rdy, k_rdy, sx_rdy, cp_rdy = sem("q_decayed"), sem("k_decayed"), sem("sx_rdy"), sem("cp_rdy")
        kt_ps, ke_rdy, ko_rdy = sem("kt_ps"), sem("ke_rdy"), sem("ko_rdy")
        upd_ps, st_rdy, o_ps, o_rd = sem("upd_ps"), sem("st_rdy"), sem("o_ps"), sem("o_rd")
        hg_in = sem("hg_in")
        osq_rdy, oss_ps, ors_rdy, og_rdy, ohh_rdy, ohl_rdy = (
            sem("osq_rdy"), sem("oss_ps"), sem("ors_rdy"), sem("og_rdy"), sem("ohh_rdy"), sem("ohl_rdy"))

        outs_mm = sem("outs_mm")
        hidf_rdy, hidh_rdy, hidl_rdy = sem("hidf_rdy"), sem("hidh_rdy"), sem("hidl_rdy")
        hid0, _n = {}, 2
        for s in segs:
            if "_in" in s.name:
                hid0[s.name] = _n
                _n += s.n * s.act
        squared0, _n = {}, 0
        for s in segs:
            if s.name.startswith("mlp") and "_in" in s.name:
                squared0[s.name] = _n
                _n += s.n * 2
        ev_end, ea_end = (after(segs[-1])[2], after(segs[-1])[1]) if segs else (FIRST_UNITS, 0)
        apply_of = {1: 1, 2: 2, 3: 4, 4: 5, 5: 6, 6: 7, 7: 8}

        nsa_in, g_in, gw_in, gw_h, gw_l = sem("nsa_in"), sem("g_in"), sem("gw_in"), sem("gw_h"), sem("gw_l")
        gate_ps, gate_rdy = sem("gate_ps"), sem("gate_rdy")
        hn_sq, hn_ss, hn_rs, hn_n = sem("hn_sq"), sem("hn_ss"), sem("hn_rs"), sem("hn_n")
        rp_ps, rp_rdy = sem("rp_ps"), sem("rp_rdy")
        cmp_ps, cmp_pos, cmp_hid, kc_ps, kc_rdy = (sem("cmp_ps"), sem("cmp_pos_rdy"), sem("cmp_hid"),
                                                   sem("kc_ps"), sem("kc_rdy"))
        vblk0, vc_ps, vblk_rdy = sem("vblk_zero"), sem("vc_ps"), sem("vblk_rdy")
        cs_ps, cs_sub, cs_exp, cs_p, cs_t, cs_te, cs_o, cs_oe = (
            sem("cs_ps"), sem("cs_sub"), sem("cs_exp"), sem("cs_p"), sem("cs_t"), sem("cs_te"),
            sem("cs_o"), sem("cs_oe"))
        at_s, at_mx, at_e, at_t, at_te, at_o, at_og = (
            sem("at_s"), sem("at_mx"), sem("at_e"), sem("at_t"), sem("at_te"), sem("at_o"), sem("at_og"))
        ot_ps, ot_h, ot_l = sem("ot_ps"), sem("ot_h"), sem("ot_l")
        dif_in, lam_sum, lam_exp = sem("dif_in"), sem("lam_sum"), sem("lam_exp")
        df_s, df_mx, df_e, df_c, df_t, df_te, df_o, df_oe, df_ln, df_n = (
            sem("df_s"), sem("df_mx"), sem("df_e"), sem("df_c"), sem("df_t"), sem("df_te"), sem("df_o"),
            sem("df_oe"), sem("df_ln"), sem("df_n"))
        dt_ps, dt_h, dt_l = sem("dt_ps"), sem("dt_h"), sem("dt_l")
        s5_ain, s5_in, s5_pp, s5_lam, s5_r, s5_trig = (
            sem("s5_a_in"), sem("s5_bc_in"), sem("s5_params_ps"), sem("s5_lambda"), sem("s5_angle"), sem("s5_trig"))
        s5_u0p, s5_u0, s5_ugp, s5_ug = sem("s5_utok_ps"), sem("s5_utok"), sem("s5_uall_ps"), sem("s5_uall")
        s5_par = sem("s5_params")
        o_v, o_g, sb_rdy, s1_tp, sbt_rdy, s1_ip, s1_ev = (
            sem("o_v"), sem("o_g"), sem("outer_rdy"), sem("s1_tp"), sem("sbt_rdy"), sem("s1_ip"), sem("s1_ev"))
        scanned = sem("scanned")
        s2_c, s2_g, s2_gev, t_in, s2_y, s2_yev = (
            sem("s2_copies"), sem("s2_g"), sem("s2_gev"), sem("toeplitz_in"), sem("s2_y"), sem("s2_yev"))
        glu_rdy = sem("glu_rdy")
        s5_fp, s5_yadd, s5_gl = sem("s5_y_ps"), sem("s5_y_added"), sem("s5_gelu")

        block = ctx.enter_context(nc.Block())
        GROUP = 2
        NG = NH // GROUP
        POOL_GROUP = NG - 1

        def by_chunk(t, j0=0, n=CH):
            v = t[:, :, :].rearrange("p h (c j) -> p (h c) j", j=CH) if len(t.shape) == 3 else \
                t[:, :].rearrange("p (c j) -> p c j", j=CH)
            return v[:, :, j0:j0 + n]

        def head_norm_act(act, link, n0, items, first_wait=None):
            def square(i):
                n = n0 + i
                if n >= 2:
                    act.wait_ge(hn_ss, n - 1)
                nc.scalar.activation(sq[:, n % 2, :], items[i][0], ACT.Square).then_inc(hn_sq, 1)
            square(0)
            for i in range(len(items)):
                n = n0 + i
                if i + 1 < len(items):
                    square(i + 1)
                act.wait_ge(hn_ss, n + 1)
                if n >= 2:
                    act.wait_ge(hn_n, n - 1)
                link(nc.scalar.activation(xn[:, n % 2, :], ps[:, 4 + n % 2, :], ACT.Ln, scale=1.0 / 64,
                                          bias=eps_col[:, :]))
                nc.scalar.activation(xn[:, n % 2, :], xn[:, n % 2, :], ACT.Exp, scale=-0.5).then_inc(hn_rs, 1)

        def head_norm_pe(pe, n0, n_items, turns, r0):
            r = r0
            for i in range(n_items):
                n = n0 + i
                pe.wait_ge(hn_sq, n + 1)
                if n >= 2:
                    pe.wait_ge(hn_rs, n - 1)
                nc.tensor.matmul(ps[:, 4 + n % 2, :], blk64, sq[:, n % 2, :], start=True, stop=True
                                 ).then_inc(hn_ss, 1)
                if i:
                    r = rope_pe(pe, n0 + i - 1, turns[i - 1], r)
            return rope_pe(pe, n0 + n_items - 1, turns[-1], r)

        def rope_pe(pe, n, jobs, r):
            pe.wait_ge(hn_n, n + 1)
            for src, mats in jobs:
                if r >= 2:
                    pe.wait_ge(rp_rdy, r - 1)
                for k, mat in enumerate(mats):
                    bank = (0, 1, 6, 7)[2 * (r % 2) + k]
                    m = nc.tensor.matmul(ps[:, bank, :], mat, src, start=True, stop=True)
                m.then_inc(rp_ps, 1)
                r += 1
            return r

        def head_norm_dve(dve, link, n0, items, jobs, r0):
            r = [r0]

            def rope(i):
                for dst in jobs[i]:
                    dve.wait_ge(rp_ps, r[0] + 1)
                    b0, b1 = ((0, 1), (6, 7))[r[0] % 2]
                    dst, plain = dst
                    t = rope_t[:, r[0] % 2, :]
                    if plain is None:
                        link(nc.vector.tensor_tensor(t, ps[:, b1, :], sinT, ALU.mult))
                        link(nc.vector.tensor_tensor(dst, ps[:, b0, :], cosT, ALU.mult))
                    else:
                        link(nc.vector.tensor_tensor(t, ps[:, b0, :], sinT, ALU.mult))
                        link(nc.vector.tensor_tensor(dst, plain, cosT, ALU.mult))
                    nc.vector.tensor_tensor(dst, dst, t, ALU.add).then_inc(rp_rdy, 1)
                    r[0] += 1
            for i, (src, gain, dst) in enumerate(items):
                n = n0 + i
                dve.wait_ge(hn_rs, n + 1)
                nc.vector.scalar_tensor_tensor(out=dst, in0=src, scalar=gain, in1=xn[:, n % 2, :],
                                               op0=ALU.mult, op1=ALU.mult).then_inc(hn_n, 1)
                if i:
                    rope(i - 1)
            rope(len(items) - 1)

        GR = ROWS["gains"]
        qk_items = [(ksr[:, i, :], cols_b[:, GR + 2:GR + 3], ksr[:, i, :]) for i in range(2)] + [
            (kwr[:, i, :], cols_b[:, GR + 3:GR + 4], kwr[:, i, :]) for i in range(2)] + [
            (nq[:, i, :], small[:, 0:1], nq[:, i, :]) for i in range(KT)]
        qk_turns = [[(x[:, i, :], (dup[j], rotdup[j])) for j in range(2)] for x in (ksr, kwr) for i in range(2)] + [
            [(nq[:, i, :], (rotm,))] for i in range(KT)]
        qk_ropes = [[(x[:, 2 * i + j, :], None) for j in range(2)] for x in (k_sel, k_win) for i in range(2)] + [
            [(nqr[:, i, :], nq[:, i, :])] for i in range(KT)]
        N_K = 4

        def nsa_loads(act):
            act.dma_start(rope_c, a["k_rope"]).then_inc(nsa_in, 16)
            act.dma_start(nsa_c, a["k_nsa"]).then_inc(nsa_in, 16)
            act.dma_start(gw.rearrange("p (k n) -> p k n", k=KT),
                          a["nsa_w_q"][0].rearrange("(k p) n -> p k n", p=P)[:, :, D:D + 48]).then_inc(gw_in, 16)

        def cmp_loads(act):
            act.dma_start(w1k, a["cmp_w1"][0].rearrange("(m p) n -> p m n", p=P)).then_inc(g_in, 16)
            act.dma_start(w1v, a["cmp_w1"][1].rearrange("(m p) n -> p m n", p=P)).then_inc(g_in, 16)
            for h in range(2):
                act.dma_start(w2[:, 0:256].rearrange("p (k n) -> p k n", k=2)[:, :, 64 * h:64 * h + 64],
                              a["cmp_w2"][0].rearrange("(k p) n -> p k n", p=P)).then_inc(g_in, 16)
            act.dma_start(w2[:, 256:384].rearrange("p (k n) -> p k n", k=2),
                          a["cmp_w2"][1].rearrange("(k p) n -> p k n", p=P)).then_inc(g_in, 16)
            for g, i0 in ((gk, 0), (gv, 2)):
                for i in range(2):
                    for h in range(2):
                        src = kvc[64 * h:64 * h + 64, i0 + i, :]
                        act.dma_start(g[0:64, 2 * i + h, :], src).then_inc(g_in, 16)
                        act.dma_start(g[64:128, 2 * i + h, 0:T - 1], src[:, 1:T]).then_inc(g_in, 16)
        CMP_LOADS = 16 * (5 + 16)

        def nsa_pe(pe):
            pe.wait_ge(gw_l, 1)
            gh = gwh[:, :].rearrange("p (k n) -> p k n", k=KT)
            gl = gwl[:, :].rearrange("p (k n) -> p k n", k=KT)
            pe.wait_ge(ev_a, after(seg["n_q"])[1])
            for t in range(TT):
                for kt in range(KT):
                    for n, (x, w) in enumerate(((hh, gh), (hl, gh), (hh, gl))):
                        m = nc.tensor.matmul(ps[:, 2, t * 48:t * 48 + 48], x[:, kt, t * P:(t + 1) * P], w[:, kt, :],
                                             start=(kt == 0 and n == 0), stop=(kt == KT - 1 and n == 2))
            m.then_inc(gate_ps, 1)
            pe.wait_ge(nsa_in, 32)
            pe.wait_ge(ada_rdy, seg["n_kvc"].ada_seg + 1)
            r = head_norm_pe(pe, 0, N_K, qk_turns[:N_K], 0)
            pe.wait_ge(g_in, CMP_LOADS)
            pe.wait_ge(rp_rdy, r)
            for kv, (g, w1) in enumerate(((gk, w1k), (gv, w1v))):
                for nt in range(2):
                    bank = (0, 1, 6, 7)[2 * kv + nt]
                    for m in range(16):
                        w = w1[:, m, nt * P:(nt + 1) * P]
                        nc.tensor.matmul(ps[:, bank, 0:124].rearrange("p (g n) -> p g n", g=4), w,
                                         g[:, :, 2 * m:2 * m + 16 * 30 + 1:16],
                                         start=(m == 0), stop=(m == 15), skip_group_check=True)
                        c = ROWS["cmp_pos"] + 16 * kv + m
                        mt = nc.tensor.matmul(ps[:, bank, 124:125], w, cols_b[:, c:c + 1],
                                              start=False, stop=(m == 15), skip_group_check=True)
                    mt.then_inc(cmp_ps, 1)
            pe.wait_ge(cmp_hid, 2)
            pe.wait_ge(gate_rdy, 1)
            for nt in range(2):
                m = nc.tensor.matmul(ps[:, 2, 0:124], w2[:, nt * P:(nt + 1) * P], hidc[:, nt, :],
                                     start=(nt == 0), stop=(nt == 1))
            m.then_inc(kc_ps, 1)
            pe.wait_ge(cmp_hid, 4)
            for g in range(KVH):
                for nt in range(2):
                    m = nc.tensor.matmul(ps[0:31, 3, g * 64:g * 64 + 64], hidc[:, 2 + nt, g * 31:(g + 1) * 31],
                                         w2[:, 256 + nt * 64:256 + nt * 64 + 64], start=(nt == 0), stop=(nt == 1))
            m.then_inc(vc_ps, 1)
            pe.wait_ge(kc_rdy, 1)
            nc.tensor.matmul(ps[:, 4, 0:124], blk64, sq[:, 0, 0:124], start=True, stop=True).then_inc(kc_ps, 1)
            pe.wait_ge(kc_rdy, 3)
            head_norm_pe(pe, N_K, KT, qk_turns[N_K:], r)
            pe.wait_ge(vblk_rdy, 1)
            pe.wait_ge(rp_rdy, r + KT)
            for t in range(TT):
                if t:
                    pe.wait_ge(cs_sub, t)
                for h in range(16):
                    rows = slice(64 * (h % 2), 64 * (h % 2) + 64)
                    m = nc.tensor.matmul(ps[:, h % 2, h // 2 * 32:h // 2 * 32 + 32], nq[rows, h // 2, t * P:(t + 1) * P],
                                         kcT[rows, h // 4, :], start=True, stop=True)
                m.then_inc(cs_ps, 1)
                if t:
                    compressed_pv(pe, t - 1)
            compressed_pv(pe, TT - 1)
            pe.wait_ge(cs_oe, TT)
            attention_pe(pe)
            pe.wait_ge(at_og, 32)
            for kt in range(KT):
                if kt >= 4:
                    pe.wait_ge(ot_l, kt - 3)
                for t in range(TT):
                    m = nc.tensor.transpose(ps[:, kt % 4, t * P:(t + 1) * P], no[:, t, kt * P:(kt + 1) * P], ident[:, :])
                m.then_inc(ot_ps, 1)

        def compressed_pv(pe, t):
            pe.wait_ge(cs_p, t + 1)
            if t:
                pe.wait_ge(cs_te, t)
            for g in range(KVH):
                m = nc.tensor.transpose(ps[:, 6, g * P:(g + 1) * P], pbuf[:, t % 2, g * P:(g + 1) * P], ident[:, :])
            m.then_inc(cs_t, 1)
            pe.wait_ge(cs_te, t + 1)
            if t:
                pe.wait_ge(cs_oe, t)
            for g in range(KVH):
                m = nc.tensor.matmul(ps[:, 2 + g // 2, g % 2 * 256:g % 2 * 256 + 256],
                                     ptbuf[:, 0, g * P:(g + 1) * P], vblk[:, g, :], start=True, stop=True)
            m.then_inc(cs_o, 1)

        UNITS = [(t, g, br, r) for t in range(TT) for g in range(KVH) for br in range(2) for r in range(4)]
        S_BANK = (0, 1, 6, 7)

        def attention_pe(pe):
            def scores(u):
                t, g, br, r = UNITS[u]
                h, n = 4 * g + r, (t + 1) * P
                rows = slice(64 * (h % 2), 64 * (h % 2) + 64)
                if u >= 4:
                    pe.wait_ge(at_e, u - 3)
                bank = S_BANK[u % 4]
                nc.tensor.matmul(ps[:, bank, 0:n], nqr[rows, h // 2, t * P:(t + 1) * P],
                                 (k_sel, k_win)[br][rows, g, 0:n], start=True, stop=False)
                nc.tensor.matmul(ps[:, bank, n - P:n], ident[:, :], causal, start=False, stop=True
                                 ).then_inc(at_s, 1)

            def turn(u):
                t = UNITS[u][0]
                pe.wait_ge(at_e, u + 1)
                if u >= 2:
                    pe.wait_ge(at_te, u - 1)
                for kt in range(t + 1):
                    m = nc.tensor.transpose(ps[:, 2 + u % 2, kt * P:(kt + 1) * P], pbuf[:, u % 4, kt * P:(kt + 1) * P],
                                            ident[:, :])
                m.then_inc(at_t, 1)

            def values(u):
                t, g, br, r = UNITS[u]
                pe.wait_ge(at_te, u + 1)
                if r == 0 and u >= 8:
                    pe.wait_ge(at_og, u // 4 - 1)
                for kt in range(t + 1):
                    m = nc.tensor.matmul(ps[:, 4 + u // 4 % 2, r * 64:r * 64 + 64], ptbuf[:, u % 2, kt * P:(kt + 1) * P],
                                         (v_sel, v_win)[br][:, kt, g * 64:g * 64 + 64],
                                         start=(kt == 0), stop=(kt == t))
                m.then_inc(at_o, 1)
            for u in range(len(UNITS) + 3):
                if u < len(UNITS):
                    scores(u)
                if 0 <= u - 2 < len(UNITS):
                    turn(u - 2)
                if 0 <= u - 3:
                    values(u - 3)

        def nsa_act(act, link):
            act.wait_ge(gw_in, 16)
            nc.scalar.activation(gwh[:, :], gw, ACT.Copy).then_inc(gw_h, 1)
            act.wait_ge(gate_ps, 1)
            nc.scalar.activation(gates.rearrange("p t n -> p (t n)"), ps[:, 2, 0:192], ACT.Sigmoid).then_inc(gate_rdy, 1)
            act.wait_ge(ev_a, after(seg["n_kw"])[1])
            cmp_loads(act)
            head_norm_act(act, link, 0, qk_items[:N_K])
            for kv in range(2):
                for nt in range(2):
                    k = 2 * kv + nt
                    act.wait_ge(cmp_pos, k + 1)
                    nc.scalar.activation(hidc[:, k, :], ps[:, (0, 1, 6, 7)[k], 0:124], ACT.Silu,
                                         bias=small[:, 8 + k:9 + k]).then_inc(cmp_hid, 1)
            act.wait_ge(kc_ps, 1)
            act.wait_ge(hn_ss, N_K)
            nc.scalar.activation(sq[:, 0, 0:124], ps[:, 2, 0:124], ACT.Square).then_inc(kc_rdy, 1)
            act.wait_ge(kc_ps, 2)
            act.wait_ge(hn_n, N_K)
            link(nc.scalar.activation(xn[:, 0, 0:124], ps[:, 4, 0:124], ACT.Ln, scale=1.0 / 64, bias=eps_col[:, :]))
            nc.scalar.activation(xn[:, 0, 0:124], xn[:, 0, 0:124], ACT.Exp, scale=-0.5).then_inc(kc_rdy, 1)
            act.wait_ge(kc_rdy, 3)
            head_norm_act(act, link, N_K, qk_items[N_K:])
            for t in range(TT):
                act.wait_ge(cs_sub, t + 1)
                nc.scalar.activation(pbuf[:, t % 2, :], pbuf[:, t % 2, :], ACT.Exp).then_inc(cs_exp, 1)
                if t:
                    compressed_out(act, t - 1)
            compressed_out(act, TT - 1)
            for u in range(len(UNITS) + 2):
                if u < len(UNITS):
                    n = (UNITS[u][0] + 1) * P
                    act.wait_ge(at_mx, u + 1)
                    if u >= 4:
                        act.wait_ge(at_t, u - 3)
                        if u % 4 == 0 and u >= 8:
                            act.wait_ge(at_og, u // 4 - 1)
                    nc.scalar.activation(pbuf[:, u % 4, 0:n], ps[:, S_BANK[u % 4], 0:n], ACT.Exp,
                                         bias=small[:, 16 + u % 8:17 + u % 8],
                                         accum_out=small[:, 24 + u % 8:25 + u % 8]).then_inc(at_e, 1)
                if u >= 2 and EVAC_ACT(u - 2):
                    v = u - 2
                    n = (UNITS[v][0] + 1) * P
                    act.wait_ge(at_t, v + 1)
                    act.wait_ge(at_te, v)
                    if v >= 2:
                        act.wait_ge(at_o, v - 1)
                    nc.scalar.activation(ptbuf[:, v % 2, 0:n], ps[:, 2 + v % 2, 0:n], ACT.Copy).then_inc(at_te, 1)
            for kt in range(KT):
                act.wait_ge(ot_ps, kt + 1)
                nc.scalar.activation(hh[:, kt, :], ps[:, kt % 4, :], ACT.Copy).then_inc(ot_h, 1)

        EVAC_ACT = lambda u: u % 2 == 0

        def compressed_out(act, t):
            act.wait_ge(cs_o, t + 1)
            nc.scalar.activation(no[:, t, :], ps[:, 2:4, :].rearrange("p b n -> p (b n)"), ACT.Copy).then_inc(cs_oe, 1)

        def nsa_dve(dve, link):
            link(nc.vector.tensor_scalar(small[:, 0:1], cols_b[:, GR:GR + 1], 0.125, None, ALU.mult))
            dve.wait_ge(gw_h, 1)
            nc.vector.tensor_tensor(gwl[:, :], gw, gwh[:, :].bitcast(F32), ALU.subtract).then_inc(gw_l, 1)
            dve.wait_ge(nsa_in, 32)
            dve.wait_ge(ev_a, after(seg["n_q"])[1])
            head_norm_dve(dve, link, 0, qk_items[:N_K], qk_ropes[:N_K], 0)
            for k in range(4):
                dve.wait_ge(cmp_ps, k + 1)
                nc.vector.tensor_copy(small[:, 8 + k:9 + k], ps[:, (0, 1, 6, 7)[k], 124:125]).then_inc(cmp_pos, 1)
            dve.wait_ge(kc_rdy, 2)
            nc.vector.scalar_tensor_tensor(
                out=kcT[:, :, 0:31], in0=ps[:, 2, 0:124].rearrange("p (g n) -> p g n", g=4),
                scalar=cols_b[:, GR + 1:GR + 2], in1=xn[:, 0, 0:124].rearrange("p (g n) -> p g n", g=4),
                op0=ALU.mult, op1=ALU.mult).then_inc(kc_rdy, 1)
            dve.wait_ge(vc_ps, 1)
            dve.wait_ge(vblk0, 2)
            for r in range(4):
                ins = nc.vector.tensor_copy(
                    vblk[32 * r:32 * r + 31, :, 64 * r:64 * r + 64],
                    ps[0:31, 3, 0:256].rearrange("p (g n) -> p g n", g=4))
            ins.then_inc(vblk_rdy, 1)
            head_norm_dve(dve, link, N_K, qk_items[N_K:], qk_ropes[N_K:], 8)
            dve.wait_ge(gate_rdy, 1)
            for t in range(TT):
                dve.wait_ge(cs_ps, t + 1)
                if t >= 2:
                    dve.wait_ge(cs_t, t - 1)
                p = pbuf[:, t % 2, :].rearrange("p (h n) -> p h n", h=16)
                s = ps[:, 0:2, 0:256].rearrange("p q (m n) -> p q m n", n=32)
                p_by_bank = pbuf[:, t % 2, :].rearrange("p (m q n) -> p q m n", q=2, n=32)
                mask = cmpmask[:, t * 32:(t + 1) * 32].unsqueeze(1).unsqueeze(1).broadcast_to((P, 2, 8, 32))
                wide = lambda x: x.unsqueeze(2).broadcast_to((P, 16, 32))
                mx, sm = small[:, 32:48], small[:, 48:64]
                link(nc.vector.tensor_tensor(p_by_bank, s, mask, ALU.add))
                link(nc.vector.tensor_reduce(mx, p, AX.X, ALU.max))
                nc.vector.tensor_tensor(p, p, wide(mx), ALU.subtract).then_inc(cs_sub, 1)
                if t:
                    compressed_turned(dve, t - 1)
                dve.wait_ge(cs_exp, t + 1)
                link(nc.vector.tensor_reduce(sm, p, AX.X, ALU.add))
                link(nc.vector.reciprocal(sm, sm))
                link(nc.vector.scalar_tensor_tensor(out=sm, in0=sm, scalar=valid[:, t:t + 1], in1=gates[:, t, 0:16],
                                                    op0=ALU.mult, op1=ALU.mult))
                nc.vector.tensor_tensor(p, p, wide(sm), ALU.mult).then_inc(cs_p, 1)
            compressed_turned(dve, TT - 1)
            dve.wait_ge(cs_oe, TT)

            def close(grp):
                t, g, br, _ = UNITS[4 * grp]
                dve.wait_ge(at_o, 4 * grp + 4)
                rs = small[:, 24 + 4 * (grp % 2):28 + 4 * (grp % 2)]
                cf = small[:, 64:68]
                link(nc.vector.reciprocal(cf, rs))
                link(nc.vector.tensor_tensor(cf, cf, gates[:, t, 16 * (br + 1) + 4 * g:16 * (br + 1) + 4 * g + 4],
                                             ALU.mult))
                o4 = ps[:, 4 + grp % 2, 0:256].rearrange("p (ri n) -> p ri n", ri=4)
                tmp = otmp.rearrange("p (ri n) -> p ri n", ri=4)
                link(nc.vector.tensor_tensor(tmp, o4, cf.unsqueeze(2).broadcast_to((P, 4, 64)), ALU.mult))
                dst = no[:, t, g * 256:g * 256 + 256]
                nc.vector.tensor_tensor(dst, dst, otmp, ALU.add).then_inc(at_og, 1)
                dve.wait_ge(at_og, grp + 1)
            for u in range(len(UNITS) + 2):
                if u < len(UNITS):
                    n = (UNITS[u][0] + 1) * P
                    dve.wait_ge(at_s, u + 1)
                    if u >= 8:
                        dve.wait_ge(at_e, u - 7)
                    nc.vector.tensor_reduce(small[:, 16 + u % 8:17 + u % 8], ps[:, S_BANK[u % 4], 0:n], AX.X, ALU.max,
                                            negate=True).then_inc(at_mx, 1)
                if u >= 2 and not EVAC_ACT(u - 2):
                    v = u - 2
                    n = (UNITS[v][0] + 1) * P
                    dve.wait_ge(at_t, v + 1)
                    dve.wait_ge(at_te, v)
                    if v >= 2:
                        dve.wait_ge(at_o, v - 1)
                    nc.vector.tensor_copy(ptbuf[:, v % 2, 0:n], ps[:, 2 + v % 2, 0:n]).then_inc(at_te, 1)
                if u >= 7 and (u - 7) % 4 == 0:
                    close((u - 7) // 4)
            for grp in range((len(UNITS) + 1 - 7) // 4 + 1, 32):
                close(grp)
            for kt in range(KT):
                dve.wait_ge(ot_h, kt + 1)
                nc.vector.tensor_tensor(hl[:, kt, :], ps[:, kt % 4, :], hh[:, kt, :].bitcast(F32), ALU.subtract
                                        ).then_inc(ot_l, 1)

        def compressed_turned(dve, t):
            dve.wait_ge(cs_t, t + 1)
            if t:
                dve.wait_ge(cs_o, t)
            nc.vector.tensor_copy(ptbuf[:, 0, :], ps[:, 6, :]).then_inc(cs_te, 1)

        LAM_INIT = 0.2
        PAIRS = [(t, h) for t in range(TT) for h in range(NH)]
        dif_items = [(x[:, i, :], g, x[:, i, :]) for x, g in ((dq, d_small[:, 0:1]), (dk, cols_b[:, GR + 5:GR + 6]))
                     for i in range(KT)]
        dif_turns = [[(x[:, i, :], (rotm,))] for x in (dq, dk) for i in range(KT)]
        dif_ropes = [[(x[:, i, :], x[:, i, :])] for x in (dq, dk) for i in range(KT)]
        HN0, RP0 = len(qk_items), 16

        def diff_pe(pe):
            pe.wait_ge(dif_in, 32)
            boundary(pe, seg["d_out"])
            r = head_norm_pe(pe, HN0, 2 * KT, dif_turns, RP0)
            pe.wait_ge(rp_rdy, r)

            def scores(w):
                t, h = PAIRS[w]
                if w >= 2:
                    pe.wait_ge(df_e, w - 1)
                for c in range(2):
                    rows = slice(64 * c, 64 * c + 64)
                    m = nc.tensor.matmul(ps[:, (0, 6)[w % 2] + c, :], dq[rows, h, t * P:(t + 1) * P],
                                         dk[rows, h, :], start=True, stop=True)
                m.then_inc(df_s, 1)

            def turn(w):
                pe.wait_ge(df_c, w + 1)
                if w >= 2:
                    pe.wait_ge(df_te, w - 1)
                for kt in range(TT):
                    m = nc.tensor.transpose(ps[:, 2 + w % 2, kt * P:(kt + 1) * P], dc[:, w % 2, kt * P:(kt + 1) * P],
                                            ident[:, :])
                m.then_inc(df_t, 1)

            def values(w):
                t, h = PAIRS[w]
                pe.wait_ge(df_te, w + 1)
                if w >= 2:
                    pe.wait_ge(df_oe, w - 1)
                for kt in range(TT):
                    m = nc.tensor.matmul(ps[:, 4 + w % 2, 0:P], dpt[:, w % 2, kt * P:(kt + 1) * P],
                                         dv[:, kt, h * P:(h + 1) * P], start=(kt == 0), stop=(kt == TT - 1))
                m.then_inc(df_o, 1)
            for w in range(len(PAIRS) + 2):
                if w < len(PAIRS):
                    scores(w)
                if 0 <= w - 1 < len(PAIRS):
                    turn(w - 1)
                if w >= 2:
                    values(w - 2)
            pe.wait_ge(df_n, TT)
            pe.wait_ge(df_oe, len(PAIRS))
            for kt in range(KT):
                if kt >= 4:
                    pe.wait_ge(dt_l, kt - 3)
                for t in range(TT):
                    m = nc.tensor.transpose(ps[:, kt % 4, t * P:(t + 1) * P], do[:, t, kt * P:(kt + 1) * P], ident[:, :])
                m.then_inc(dt_ps, 1)
            pe.wait_ge(dt_l, KT)

        def diff_act(act, link):
            act.wait_ge(lam_sum, 1)
            nc.scalar.activation(d_small[:, 2:4], d_small[:, 4:6], ACT.Exp).then_inc(lam_exp, 1)
            act.wait_ge(ev_v, after(seg["d_v"])[2])
            head_norm_act(act, link, HN0, dif_items)

            def turned(w):
                act.wait_ge(df_t, w + 1)
                if w >= 2:
                    act.wait_ge(df_o, w - 1)
                nc.scalar.activation(dpt[:, w % 2, :], ps[:, 2 + w % 2, :], ACT.Copy).then_inc(df_te, 1)

            def out(w):
                t, h = PAIRS[w]
                act.wait_ge(df_o, w + 1)
                link(nc.scalar.activation(do[:, t, h * P:(h + 1) * P], ps[:, 4 + w % 2, 0:P], ACT.Copy))
                nc.scalar.activation(d_sq, do[:, t, h * P:(h + 1) * P], ACT.Square,
                                     accum_out=d_small[:, 64 + w:65 + w]).then_inc(df_oe, 1)
                act.wait_ge(df_oe, w + 1)
            for w in range(len(PAIRS) + 2):
                if w < len(PAIRS):
                    act.wait_ge(df_mx, w + 1)
                    if w >= 2:
                        act.wait_ge(df_c, w - 1)
                    for c in range(2):
                        i = 2 * (w % 2) + c
                        ins = nc.scalar.activation(dp[:, w % 2, c, :], ps[:, (0, 6)[w % 2] + c, :], ACT.Exp,
                                                   bias=d_small[:, 8 + i:9 + i], accum_out=d_small[:, 12 + i:13 + i])
                    ins.then_inc(df_e, 1)
                if 0 <= w - 1 < len(PAIRS):
                    turned(w - 1)
                if w >= 2:
                    out(w - 2)
            link(nc.scalar.activation(d_small[:, 64:96], d_small[:, 64:96], ACT.Ln, scale=1.0 / P, bias=eps_col[:, :]))
            nc.scalar.activation(d_small[:, 64:96], d_small[:, 64:96], ACT.Exp, scale=-0.5).then_inc(df_ln, 1)
            for kt in range(KT):
                act.wait_ge(dt_ps, kt + 1)
                nc.scalar.activation(hh[:, kt, :], ps[:, kt % 4, :], ACT.Copy, scale=d_small[:, 1:2]).then_inc(dt_h, 1)

        def diff_dve(dve, link):
            dve.wait_ge(dif_in, 32)
            lv = lam_vec.rearrange("p (a b n) -> p a b n", a=2, b=2)
            pr = lam_tmp.rearrange("p (a n) -> p a n", a=2)
            link(nc.vector.tensor_tensor(pr, lv[:, :, 0, :], lv[:, :, 1, :], ALU.mult))
            nc.vector.tensor_reduce(d_small[:, 4:6], pr, AX.X, ALU.add).then_inc(lam_sum, 1)
            s = ROWS["attn_subln_2"]
            nc.vector.tensor_scalar(d_small[:, 1:2], cols_b[:, s:s + 1], 1.0 - LAM_INIT, None, ALU.mult
                                    ).then_inc(lam_sum, 1)
            link(nc.vector.tensor_scalar(d_small[:, 0:1], cols_b[:, GR + 4:GR + 5], 0.125, None, ALU.mult))
            dve.wait_ge(lam_exp, 1)
            link(nc.vector.scalar_tensor_tensor(out=d_small[:, 6:7], in0=d_small[:, 3:4], scalar=-LAM_INIT,
                                                in1=d_small[:, 2:3], op0=ALU.add, op1=ALU.subtract))
            dve.wait_ge(ev_a, after(seg["d_k"])[1])
            head_norm_dve(dve, link, HN0, dif_items, dif_ropes, RP0)
            for w in range(len(PAIRS) + 1):
                if w:
                    v = w - 1
                    i = 2 * (v % 2)
                    dve.wait_ge(df_e, v + 1)
                    rs = d_small[:, 16 + i:18 + i]
                    link(nc.vector.reciprocal(rs, d_small[:, 12 + i:14 + i]))
                    link(nc.vector.tensor_scalar(dp[:, v % 2, 1, :], dp[:, v % 2, 1, :], rs[:, 1:2],
                                                 d_small[:, 6:7], ALU.mult, ALU.mult))
                    if v >= 2:
                        dve.wait_ge(df_t, v - 1)
                    nc.vector.scalar_tensor_tensor(out=dc[:, v % 2, :], in0=dp[:, v % 2, 0, :], scalar=rs[:, 0:1],
                                                   in1=dp[:, v % 2, 1, :], op0=ALU.mult, op1=ALU.add
                                                   ).then_inc(df_c, 1)
                if w < len(PAIRS):
                    dve.wait_ge(df_s, w + 1)
                    if w >= 2:
                        dve.wait_ge(df_e, w - 1)
                    i = 2 * (w % 2)
                    b = (0, 6)[w % 2]
                    nc.vector.tensor_reduce(d_small[:, 8 + i:10 + i], ps[:, b:b + 2, :], AX.X, ALU.max,
                                            negate=True).then_inc(df_mx, 1)
            dve.wait_ge(df_ln, 1)
            for t in range(TT):
                x = do[:, t, :].rearrange("p (h n) -> p h n", h=NH)
                r = d_small[:, 64 + 8 * t:72 + 8 * t].unsqueeze(2).broadcast_to((P, NH, P))
                nc.vector.tensor_tensor(x, x, r, ALU.mult).then_inc(df_n, 1)
            for kt in range(KT):
                dve.wait_ge(dt_h, kt + 1)
                nc.vector.scalar_tensor_tensor(out=hl[:, kt, :], in0=ps[:, kt % 4, :], scalar=d_small[:, 1:2],
                                               in1=hh[:, kt, :].bitcast(F32), op0=ALU.mult, op1=ALU.subtract
                                               ).then_inc(dt_l, 1)

        K5 = 7
        M5 = 6
        DONE2 = 2

        def s5_loads(act):
            for n, name in enumerate(("ssm_a_re_2", "ssm_a_im_2")):
                act.dma_start(a_raw[:, n, :].rearrange("g (d p) -> g d p", d=2),
                              a[name][0].rearrange("d g p -> g d p")).then_inc(s5_ain, 16)
            for d in range(2):
                act.dma_start(log_dt[64 * d:64 * d + 64, :], a["ssm_log_dt_2"][0, d:d + 1, :].broadcast_to((64, NG5))
                              ).then_inc(s5_ain, 16)
            for n, name in enumerate(("ssm_b_re_2", "ssm_b_im_2")):
                act.dma_start(bc_raw[:, n, :].rearrange("g (d m) -> g d m", d=2),
                              a[name][0].rearrange("d g p h -> g d (p h)")).then_inc(s5_in, 16)
            for n, name in enumerate(("ssm_c_re_2", "ssm_c_im_2")):
                for d in range(2):
                    act.dma_start(bc_raw[:, 2 + n, :].rearrange("g (h d p) -> g d h p", d=2, h=GH)[:, d, :, :],
                                  a[name][0, d]).then_inc(s5_in, 16)

        def s5_pe(pe):
            i64 = ident[0:64, 0:64]
            pe.nop().then_inc(s1_tp, DONE2)
            pe.nop().then_inc(s1_ip, DONE2)
            pe.nop().then_inc(s2_g, DONE2)
            pe.nop().then_inc(s2_y, DONE2)
            boundary(pe, seg["s_glu"])
            pe.wait_ge(s5_ain, 64)
            for n in range(2):
                m = nc.tensor.transpose(ps[:, 6, n * 64:n * 64 + 64], a_raw[:, n, :], i64)
            m.then_inc(s5_pp, 1)
            for kt in range(KT):
                pe.wait_ge(xn_rdy, KT * K5 + kt + 1)
                if kt >= 3:
                    pe.wait_ge(s5_u0, kt - 2)
                for t in range(L8):
                    m = nc.tensor.transpose(ps[0:64, 2 * (kt % 3) + t // 4, t % 4 * P:(t % 4 + 1) * P],
                                            uT[:, kt, t:T:L8], ident[:, :])
                m.then_inc(s5_u0p, 1)
            pe.wait_ge(s5_u0, KT)
            for r in range(KT):
                if r >= 6:
                    pe.wait_ge(s5_ug, r - 5)
                for i in range(8):
                    m = nc.tensor.transpose(ps[:, r % 6, i * 64:i * 64 + 64],
                                            u_tok[:, 8 * r + i, :, :].rearrange("c t h -> c (t h)"), i64)
                m.then_inc(s5_ugp, 1)
            pe.wait_ge(s5_in, 96)
            pe.wait_ge(s5_ug, KT)
            pe.wait_ge(s5_lam, 1)
            pe.wait_ge(rstd_rdy, M5 + 1)
            for n in range(4):
                for h in range(GH):
                    src = bc_raw[:, n, :].rearrange("g (m h) -> g m h", h=GH)[:, :, h] if n < 2 else \
                        bc_raw[:, n, h * P:(h + 1) * P]
                    m = nc.tensor.transpose(ps[:, 2 * n + h // 8, h % 8 * 64:h % 8 * 64 + 64], src, i64)
                m.then_inc(s5_pp, 1)
            pe.wait_ge(s5_par, 1)

            def chunk_sums(b, p):
                pe.wait_ge(sb_rdy, b + (DONE2 + 1))
                pe.wait_ge(sbt_rdy, b + 1)
                for ri in range(2):
                    for g in range(4):
                        m = nc.tensor.transpose(ps[:, 2 * p + ri, g * P:(g + 1) * P], sb_[:, p, ri, g, :], ident[:, :])
                m.then_inc(s1_tp, 1)
                pe.wait_ge(sbt_rdy, b + (DONE2 + 1))
                pe.wait_ge(s1_ev, b + 1)
                for ri in range(2):
                    for g in range(4):
                        c = (4 * ri + g) * NC8
                        m = nc.tensor.matmul(ps[:, 4 + p, c:c + NC8], sbt[:, p, ri, g, :],
                                             u_all[:, bass.ds(b * 4 + g, 1), :].rearrange("p g c -> p (g c)"), start=True, stop=True)
                m.then_inc(s1_ip, 1)
            with pe.Fori(0, NB5 // 2) as i:
                for p in range(2):
                    chunk_sums(i * 2 + p, p)

            def kernels(b, p):
                pe.wait_ge(sb_rdy, b + (NB5 + DONE2 + 1))
                pe.wait_ge(s2_c, b + 1)
                pe.wait_ge(s2_gev, b + 1)
                for g in range(4):
                    for ri in range(2):
                        nc.tensor.matmul(ps[0:GH, 2 * p, g * P:g * P + GH], bb[:, p, ri, g, :],
                                         c_mat[:, ri, bass.ds(b * 4 + g, 1), :].rearrange("p g h -> p (g h)"),
                                         start=(ri == 0), stop=(ri == 1))
                    for ri in range(2):
                        nc.tensor.matmul(ps[0:GH, 2 * p, g * P + GH:(g + 1) * P], bb[0:64, p, ri, g, :],
                                         cp[0:64, p, ri, g, 0:P - GH], start=(ri == 0), stop=(ri == 1))
                    for ri in range(2):
                        m = nc.tensor.matmul(ps[0:GH, 2 * p + 1, g * 112:(g + 1) * 112], bb[64:P, p, ri, g, :],
                                             cp[64:P, p, ri, g, GH:P], start=(ri == 0), stop=(ri == 1))
                m.then_inc(s2_g, 1)

            def outputs(b, p):
                pe.wait_ge(t_in, (b + 1) * (16 * L8))
                pe.wait_ge(s2_yev, b + 1)
                for g in range(4):
                    y = ps[0:NC8, 4 + p, g * P:(g + 1) * P]
                    nc.tensor.matmul(y, ub[:, p, g, :], toep[:, p, g, :], start=True, stop=False)
                    for ri in range(2):
                        m = nc.tensor.matmul(y, hb[:, p, ri, g, :], cp[:, p, ri, g, :], start=False, stop=(ri == 1))
                m.then_inc(s2_y, 1)
            kernels(0, 0)
            with pe.Fori(0, NB5 // 2 - 1) as i:
                for p in range(2):
                    kernels(i * 2 + (p + 1), 1 - p)
                    outputs(i * 2 + p, p)
            kernels(NB5 - 1, 1)
            outputs(NB5 - 2, 0)
            outputs(NB5 - 1, 1)
            pe.wait_ge(s2_yev, NB5 + DONE2)
            for kt in range(KT):
                if kt >= 4:
                    pe.wait_ge(s5_yadd, kt - 3)
                for t in range(L8):
                    m = nc.tensor.transpose(ps[:, kt % 4, t * NC8:(t + 1) * NC8], y_tok[:, t, kt * P:(kt + 1) * P], i64)
                m.then_inc(s5_fp, 1)
            pe.wait_ge(s5_yadd, KT)

        def s5_act(act, link):
            act.nop().then_inc(sbt_rdy, DONE2)
            act.nop().then_inc(s1_ev, DONE2)
            act.nop().then_inc(s2_gev, DONE2)
            act.nop().then_inc(s2_yev, DONE2)
            dt, x, r, s, sh, e = (par5[i] for i in (0, 3, 4, 6, 7, 8))
            act.wait_ge(s5_ain, 64)
            nc.scalar.activation(dt, log_dt, ACT.Exp).then_inc(s5_trig, 1)
            act.wait_ge(s5_r, 1)
            nc.scalar.activation(e, x, ACT.Exp)
            nc.scalar.activation(s, r, ACT.Sin)
            nc.scalar.activation(sh, r, ACT.Sin, scale=0.5).then_inc(s5_trig, 1)
            for kt in range(KT):
                act.wait_ge(s5_u0p, kt + 1)
                if kt == 0:
                    act.wait_ge(s5_pp, 1)
                src = ps[0:NC8, 2 * (kt % 3):2 * (kt % 3) + 2, :].rearrange("c b (t g h) -> c (b t) g h", t=4, h=GH)
                nc.scalar.activation(u_tok[:, 8 * kt:8 * kt + 8, :, :].rearrange("c g t h -> c t g h"), src, ACT.Copy
                                     ).then_inc(s5_u0, 1)
            for r_ in range(KT):
                act.wait_ge(s5_ugp, r_ + 1)
                nc.scalar.activation(u_all[:, 8 * r_:8 * r_ + 8, :].rearrange("p g c -> p (g c)"), ps[:, r_ % 6, :],
                                     ACT.Copy).then_inc(s5_ug, 1)

            def chunk_sums(b, p):
                act.wait_ge(s1_tp, b + (DONE2 + 1))
                act.wait_ge(s1_ip, b + 1)
                for ri in range(2):
                    ins = nc.scalar.activation(sbt[:, p, ri, :, :].rearrange("p g n -> p (g n)"), ps[:, 2 * p + ri, :], ACT.Copy)
                ins.then_inc(sbt_rdy, 1)
                act.wait_ge(s1_ip, b + (DONE2 + 1))
                src = ps[:, 4 + p, :].rearrange("p (ri g c) -> p ri g c", ri=2, g=4)
                for ri in range(2):
                    nc.scalar.activation(H[0:64, ri, bass.ds(b * 4, 4), 1:NC8], src[0:64, ri, :, 0:NC8 - 1], ACT.Copy)
                    ins = nc.scalar.activation(H[64:P, ri, bass.ds(b * 4, 4), 1:NC8], src[64:P, ri, :, NC8 - 1:0:-1], ACT.Copy)
                ins.then_inc(s1_ev, 1)
            act.wait_ge(s5_pp, 5)
            with act.Fori(0, NB5 // 2) as i:
                for p in range(2):
                    chunk_sums(i * 2 + p, p)

            def operands(b, p):
                act.wait_ge(s2_g, b + 1)
                act.wait_ge(s2_y, b + 1)
                nc.scalar.activation(bb[:, p, :, :, :], b_bar[:, :, bass.ds(b * 4, 4), :], ACT.Copy)
                nc.scalar.activation(ub[:, p, :, :], u_all[:, bass.ds(b * 4, 4), :], ACT.Copy)
                for ri in range(2):
                    nc.scalar.activation(hb[0:64, p, ri, :, :], H[0:64, ri, bass.ds(b * 4, 4), :], ACT.Copy)
                    ins = nc.scalar.activation(hb[64:P, p, ri, :, ::-1], H[64:P, ri, bass.ds(b * 4, 4), :], ACT.Copy)
                ins.then_inc(s2_c, 1)
                act.wait_ge(s2_g, b + (DONE2 + 1))
                if not (isinstance(b, int) and b == 0):
                    act.wait_ge(t_in, b * (16 * L8))
                nc.scalar.activation(g_sb[:, :, 112:240], ps[0:GH, 2 * p, :].rearrange("p (g n) -> p g n", g=4), ACT.Copy)
                nc.scalar.activation(g_sb[:, :, 0:112], ps[0:GH, 2 * p + 1, 0:448].rearrange("p (g n) -> p g n", g=4),
                                     ACT.Copy).then_inc(s2_gev, 1)

            def y_out(b, p):
                act.wait_ge(s2_y, b + (DONE2 + 1))
                nc.scalar.activation(y_tok[:, :, bass.ds(b * 64, 64)].rearrange("c t (g h) -> c t g h", g=4),
                                     ps[0:NC8, 4 + p, :].rearrange("c (g t h) -> c t g h", g=4, h=GH), ACT.Copy
                                     ).then_inc(s2_yev, 1)
            act.wait_ge(scanned, 4 * (NC8 - 1))
            act.wait_ge(s1_ip, NB5 + DONE2)
            operands(0, 0)
            with act.Fori(0, NB5 // 2 - 1) as i:
                for p in range(2):
                    operands(i * 2 + (p + 1), 1 - p)
                    y_out(i * 2 + p, p)
            operands(NB5 - 1, 1)
            y_out(NB5 - 2, 0)
            y_out(NB5 - 1, 1)
            for kt in range(KT):
                act.wait_ge(s5_yadd, kt + 1)
                if kt >= 2:
                    act.wait_ge(hl_rdy, KT * K5 + kt - 1)
                nc.scalar.activation(xn[:, kt % 2, :], sq[:, kt % 2, :], ACT.Gelu_apprx_tanh).then_inc(s5_gl, 1)
                act.wait_ge(s5_gl, kt + 1)
                nc.scalar.activation(hh[:, kt, :], xn[:, kt % 2, :], ACT.Copy).then_inc(hh_rdy, 1)

        def s5_toeplitz(sp):
            with sp.Fori(0, NB5 // 2) as i:
                for p in range(2):
                    done = sp.snap(i * 2 + (p + DONE2 + 1))
                    sp.wait_ge(s2_gev, done)
                    for t in range(L8):
                        sp.dma_start(toep[GH * t:GH * t + GH, p, :, :], g_sb[:, :, (7 - t) * GH:(7 - t) * GH + P]
                                     ).then_inc(t_in, 16)

        def by_group(pw_, x, b):
            return ([pw_[:, ri, bass.ds(b * 4, 4), :].unsqueeze(3).broadcast_to((P, 4, L8, GH)) for ri in range(2)],
                    [x[:, ri, bass.ds(b * 4, 4), :].unsqueeze(2).broadcast_to((P, 4, L8, GH)) for ri in range(2)])

        def block4(t):
            return t.rearrange("p (g t h) -> p g t h", g=4, h=GH)

        def outer_pool(pool, pw_, x, b, tmp, n0, free):
            pool.wait_ge(sb_rdy, b + free)
            w, m = by_group(pw_, x, b)
            nc.gpsimd.tensor_tensor(block4(tmp[:, 0:512]), w[1], m[1], ALU.mult)
            nc.gpsimd.tensor_tensor(block4(tmp[:, 512:1024]), w[1], m[0], ALU.mult).then_inc(o_g, 1)

        def outer_dve(dve, pw_, x, b, p, tmp, n0, used):
            dve.wait_ge(used, b + 1)
            w, m = by_group(pw_, x, b)
            dst = [sb_[:, p, ri, :, :].rearrange("p g n -> p (g n)") for ri in range(2)]
            for ri in range(2):
                nc.vector.tensor_tensor(block4(dst[ri]), w[0], m[ri], ALU.mult).then_inc(o_v, 1)
            dve.wait_ge(o_g, b + (n0 + 1))
            dve.wait_ge(o_v, b * 2 + (2 * n0 + 2))
            nc.vector.tensor_tensor(dst[0], dst[0], tmp[:, 0:512], ALU.subtract)
            nc.vector.tensor_tensor(dst[1], dst[1], tmp[:, 512:1024], ALU.add).then_inc(sb_rdy, 1)

        def s5_pool(pool):
            pool.wait_ge(s5_pp, 5)
            nc.gpsimd.memset(H[:, :, :, 0:1], 0.0).then_inc(pool_set, 1)
            pool.wait_ge(s5_par, 2)
            with pool.Fori(0, NB5 // 2) as i:
                for p in range(2):
                    outer_pool(pool, pw_in, b_bar, i * 2 + p, tmp_in[:, p, :], 0, 1)
            pool.wait_ge(s1_tp, NB5 + DONE2)
            pool.wait_ge(scanned, 4 * (NC8 - 1))
            with pool.Fori(0, NB5 // 2) as i:
                for p in range(2):
                    outer_pool(pool, pw_out, c_mat, i * 2 + p, tmp_out, NB5, NB5 + DONE2)

        def s5_dve(dve, link):
            tt, ts, stt = nc.vector.tensor_tensor, nc.vector.tensor_scalar, nc.vector.scalar_tensor_tensor
            dve.nop().then_inc(sb_rdy, DONE2)
            dve.nop().then_inc(scanned, 4)
            dve.wait_ge(rstd_rdy, M5 + 1)
            dve.wait_ge(mm, seg["s_glu"].mm0)
            r0 = ROWS["norm_mix_2"] + 8
            for kt in range(KT):
                stt(out=uT[:, kt, :], in0=xT[:, kt, :], scalar=cols_b[:, r0 + kt:r0 + kt + 1], in1=rstd[:, :],
                    op0=ALU.mult, op1=ALU.mult).then_inc(xn_rdy, 1)
            (dt, lr, li, x, y, k, s, sh, e, xc, q, m, amr, den, wr) = par5
            dve.wait_ge(s5_pp, 1)
            dve.wait_ge(s5_ain, 64)
            nc.vector.tensor_copy(s5_area[:, 23680 + 64:23680 + 192], ps[:, 6, 0:128]).then_inc(s5_lam, 1)
            dve.wait_ge(s5_lam, 1)
            dve.wait_ge(s5_trig, 1)
            tt(x, lr, dt, ALU.mult)
            link(tt(y, li, dt, ALU.mult))
            link(ts(k, y, 1 / (2 * np.pi), 12582912.0, ALU.mult, ALU.add))
            link(ts(k, k, 12582912.0, None, ALU.subtract))
            c1, c2 = 6.28125, float(np.float32(0.0019350051879882812))
            c3 = 2 * np.pi - c1 - c2
            for c in (c1, c2, c3):
                link(stt(out=y, in0=k, scalar=-c, in1=y, op0=ALU.mult, op1=ALU.add))
            ts(y, y, 3.1415925, -3.1415925, ALU.min, ALU.max).then_inc(s5_r, 1)
            link(ts(xc, x, 0.25, -0.25, ALU.min, ALU.max))
            tt(m, xc, x, ALU.is_equal)
            link(ts(q, xc, 1.0 / 7, 1.0, ALU.mult, ALU.add))
            for n in range(6, 1, -1):
                link(stt(out=q, in0=q, scalar=1.0 / n, in1=xc, op0=ALU.mult, op1=ALU.mult))
                link(ts(q, q, 1.0, None, ALU.add))
            link(tt(q, q, xc, ALU.mult))
            dve.wait_ge(s5_trig, 2)
            link(ts(e, e, -1.0, None, ALU.add))
            link(tt(q, q, e, ALU.subtract))
            link(tt(q, q, m, ALU.mult))
            link(tt(e, e, q, ALU.add))
            link(tt(sh, sh, sh, ALU.mult))
            ar, ai = pw[:, 0, 1, :], pw[:, 1, 1, :]
            link(ts(q, sh, -2.0, 1.0, ALU.mult, ALU.add))
            link(tt(q, e, q, ALU.mult))
            link(stt(out=amr, in0=sh, scalar=-2.0, in1=q, op0=ALU.mult, op1=ALU.add))
            link(stt(out=ai, in0=e, scalar=1.0, in1=s, op0=ALU.add, op1=ALU.mult))
            nc.vector.tensor_scalar(ar, amr, 1.0, None, ALU.add)
            nc.vector.memset(pw[:, 0, 0, :], 1.0)
            nc.vector.memset(pw[:, 1, 0, :], 0.0)
            tt(q, lr, lr, ALU.mult)
            link(tt(den, li, li, ALU.mult))
            link(tt(den, den, q, ALU.add))
            link(nc.vector.reciprocal(den, den))
            wi = m
            tt(wr, amr, lr, ALU.mult)
            tt(wi, ai, lr, ALU.mult)
            link(tt(q, ai, li, ALU.mult))
            link(tt(wr, wr, q, ALU.add))
            link(tt(q, amr, li, ALU.mult))
            link(tt(wi, wi, q, ALU.subtract))
            tt(wr, wr, den, ALU.mult)
            link(tt(wi, wi, den, ALU.mult))
            t1, t2 = bb_tmp[:, 0:256], bb_tmp[:, 256:512]
            for base, n in ((1, 1), (2, 2), (4, 4)):
                c, d = base + 1, base + 1 + n
                xr, xi = (pw[:, ri, 1:1 + n, :] for ri in range(2))
                br, bi = (pw[:, ri, base:base + 1, :].broadcast_to((P, n, NG5)) for ri in range(2))
                u1, u2 = (t[:, 0:64 * n].rearrange("p (k g) -> p k g", k=n) for t in (t1, t2))
                tt(u1, xi, bi, ALU.mult)
                tt(u2, xi, br, ALU.mult)
                tt(pw[:, 0, c:d, :], xr, br, ALU.mult)
                link(tt(pw[:, 1, c:d, :], xr, bi, ALU.mult))
                tt(pw[:, 0, c:d, :], pw[:, 0, c:d, :], u1, ALU.subtract)
                link(tt(pw[:, 1, c:d, :], pw[:, 1, c:d, :], u2, ALU.add))
            for ri in range(2):
                for rows, i_in, i_out in ((slice(0, 64), slice(7, None, -1), slice(1, 9)),
                                          (slice(64, P), slice(0, 8), slice(8, 0, -1))):
                    nc.vector.tensor_copy(pw_in[rows, ri, :, :], pw[rows, ri, i_in, :].rearrange("p k g -> p g k"))
                    src = pw[rows, ri, i_out, :].rearrange("p k g -> p g k")
                    if ri:
                        ts(pw_out[rows, ri, :, :], src, -1.0, None, ALU.mult)
                    else:
                        nc.vector.tensor_copy(pw_out[rows, ri, :, :], src)
            nc.vector.tensor_scalar(a8i[:, 1, :], pw[:, 1, 8, :], -1.0, None, ALU.mult)
            nc.vector.tensor_copy(a8i[:, 0, :], pw[:, 1, 8, :])
            d0 = ROWS["ssm_d_2"]
            link(tt(gains_a[:, 5, :], cols_b[:, r0:r0 + 8], cols_b[:, d0:d0 + 8], ALU.mult))
            dve.wait_ge(s5_pp, 5)
            by_g = lambda x_: x_.rearrange("p g h -> p h g")
            inp = [ps[:, 2 * n:2 * n + 2, :].rearrange("p b (h g) -> p (b h) g", g=NG5) for n in range(4)]
            nc.vector.tensor_copy(by_g(c_mat[:, 0, :, :]), inp[2])
            ts(by_g(c_mat[:, 1, :, :]), inp[3], -1.0, None, ALU.mult)
            wide = lambda w: w.unsqueeze(1).broadcast_to((P, GH, NG5))
            tmp = bb_tmp.rearrange("p (h g) -> p h g", h=GH)
            tt(by_g(b_bar[:, 0, :, :]), inp[0], wide(wr), ALU.mult)
            tt(by_g(b_bar[:, 1, :, :]), inp[0], wide(wi), ALU.mult)
            link(tt(tmp, inp[1], wide(wi), ALU.mult))
            link(tt(by_g(b_bar[:, 0, :, :]), by_g(b_bar[:, 0, :, :]), tmp, ALU.subtract))
            tt(tmp, inp[1], wide(wr), ALU.mult).then_inc(s5_par, 1)
            dve.wait_ge(s5_par, 1)
            tt(by_g(b_bar[:, 1, :, :]), by_g(b_bar[:, 1, :, :]), tmp, ALU.add).then_inc(s5_par, 1)
            dve.wait_ge(s5_par, 2)
            dve.wait_ge(s5_u0p, KT)
            with dve.Fori(0, NB5 // 2) as i:
                for p in range(2):
                    outer_dve(dve, pw_in, b_bar, i * 2 + p, p, tmp_in[:, p, :], 0, s1_tp)
            dve.wait_ge(s1_ev, NB5 + DONE2)
            dve.wait_ge(pool_set, 4)
            Hs = H.rearrange("p ri g s -> p s ri g")
            a8r = pw[:, 0:1, 8, :].broadcast_to((P, 2, NG5)).unsqueeze(1)
            with dve.Fori(0, NC8 // 2 - 1) as i:
                for u in range(2):
                    n = i * 2 + u
                    dve.wait_ge(scanned, n * 4 + 4)
                    prev, cur = Hs[:, bass.ds(n + 1, 1), :, :], Hs[:, bass.ds(n + 2, 1), :, :]
                    ta, tb = scan_t[:, 0:1, :, :], scan_t[:, 1:2, :, :]
                    tt(ta, prev, a8r, ALU.mult).then_inc(scanned, 1)
                    tt(tb[:, :, ::-1, :], prev, a8i.unsqueeze(1), ALU.mult).then_inc(scanned, 1)
                    dve.wait_ge(scanned, n * 4 + 5)
                    tt(cur, cur, ta, ALU.add).then_inc(scanned, 1)
                    dve.wait_ge(scanned, n * 4 + 7)
                    tt(cur, cur, tb, ALU.add).then_inc(scanned, 1)
            dve.wait_ge(s1_ip, NB5 + DONE2)
            with dve.Fori(0, NB5 // 2) as i:
                for p in range(2):
                    outer_dve(dve, pw_out, c_mat, i * 2 + p, p, tmp_out, NB5, s2_y)
            for kt in range(KT):
                if kt >= 2:
                    dve.wait_ge(s5_gl, kt - 1)
                z = sq[:, kt % 2, :]
                link(stt(out=z, in0=xT[:, kt, :], scalar=gains_a[:, 5, kt:kt + 1], in1=rstd[:, :],
                         op0=ALU.mult, op1=ALU.mult))
                dve.wait_ge(s5_fp, kt + 1)
                z8 = z.rearrange("p (c t) -> p c t", t=L8)
                tt(z8, z8, ps[:, kt % 4, :].rearrange("p (t c) -> p c t", t=L8), ALU.add).then_inc(s5_yadd, 1)
                if kt:
                    s5_low(dve, kt - 1)
            s5_low(dve, KT - 1)

        def s5_low(dve, kt):
            dve.wait_ge(hh_rdy, KT * K5 + kt + 1)
            nc.vector.tensor_tensor(hl[:, kt, :], xn[:, kt % 2, :], hh[:, kt, :].bitcast(F32), ALU.subtract
                                    ).then_inc(hl_rdy, 1)

        def hgrn_pool(pool):
            g = POOL_GROUP
            for d in range(CH):
                if d == 0:
                    pool.wait_ge(band_zero, 32)
                if d:
                    pool.wait_ge(lag_rdy, d)
                else:
                    pool.wait_ge(ev_a, after(seg["h_f"])[1])
                if d:
                    pool.wait_ge(band_mm, d * NG)
                src = kT if d == 0 else scr1
                w = by_chunk(src, 0, CH - d)[:, g * GROUP * NCH:, :]
                nc.gpsimd.tensor_tensor(by_chunk(scr2, 0, CH - d)[:, g * GROUP * NCH:, :], w,
                                        by_chunk(qT, d, CH - d)[:, g * GROUP * NCH:, :], ALU.mult
                                        ).then_inc(prod_g, 1)
            pool.wait_ge(band_mm, CH * NG)
            n = 0
            nc.gpsimd.memset(by_chunk(scr2, CH - 1, 1), 1.0).then_inc(sx_rdy, 1)
            for j in range(CH - 2, -1, -1):
                n += 1
                pool.wait_ge(sx_rdy, n)
                nc.gpsimd.tensor_tensor(by_chunk(scr2, j, 1), by_chunk(scr2, j + 1, 1),
                                        by_chunk(fT, j + 1, 1), ALU.mult).then_inc(sx_rdy, 1)
        def hgrn_act_states(act):
            act.dma_start(sel[:, :], a["k_sel"]).then_inc(hg_in, 16)
            act.dma_start(evenodd[:, :], a["k_evenodd"]).then_inc(hg_in, 16)
            act.wait_ge(bandT_sb, 1)
            act.wait_ge(band_zero, 32)
            dst = band_dram.ap()[:, 0:P * (PITCH + 1)].rearrange("m (s n) -> s m n", n=PITCH + 1)[:, :, 0:CH]
            act.dma_start(dst, bandT.rearrange("p t (h d) -> p (t h) d", h=NH)).then_inc(band_out, 16)
            act.wait_ge(band_out, 16)
            act.wait_ge(k_rdy, 1)
            src = band_dram.ap()[:, 0:P * PITCH].rearrange("m (s n) -> s m n", n=PITCH)[:, :, 0:P]
            act.dma_start(fT[:, :, :].rearrange("p h (x n) -> p (h x) n", n=P), src).then_inc(band_in, 16)
            act.wait_ge(hg_in, 32)
            for n in range(TT * 2):
                act.wait_ge(kt_ps, n + 1)
                if n == 0:
                    act.wait_ge(k_rdy, 1)
                act.wait_ge(ke_rdy, n + 1)
                nc.scalar.activation(scr2[:, n * T:(n + 1) * T], ps[:, n % 4, :], ACT.Copy,
                                     scale=evenodd[:, 1:2]).then_inc(ko_rdy, 1)
            for t in range(TT):
                act.wait_ge(o_ps, t + 1)
                if t == 0:
                    act.wait_ge(kt_ps, TT * 2)
                b = 4 * (t % 2)
                nc.scalar.activation(kT[:, :, t * P:(t + 1) * P],
                                     ps[:, b:b + 2, :].rearrange("p b (h n) -> p (b h) n", n=P),
                                     ACT.Copy).then_inc(o_rd, 1)

        def hgrn_act_out(act, link):
            act.wait_ge(o_rd, TT)
            for h in range(NH):
                if h >= 2:
                    act.wait_ge(oss_ps, h - 1)
                nc.scalar.activation(sq[:, h % 2, :], kT[:, h, :], ACT.Square).then_inc(osq_rdy, 1)
                act.wait_ge(oss_ps, h + 1)
                if h >= 2:
                    act.wait_ge(og_rdy, h - 1)
                link(nc.scalar.activation(xn[:, h % 2, :], ps[:, 2 + h % 2, :], ACT.Ln, scale=1.0 / P,
                                          bias=eps_col[:, :]))
                nc.scalar.activation(xn[:, h % 2, :], xn[:, h % 2, :], ACT.Exp, scale=-0.5).then_inc(ors_rdy, 1)
                if h:
                    act.wait_ge(og_rdy, h)
                    nc.scalar.activation(hh[:, h - 1, :], gT[:, h - 1, :], ACT.Copy).then_inc(ohh_rdy, 1)
            act.wait_ge(og_rdy, NH)
            nc.scalar.activation(hh[:, NH - 1, :], gT[:, NH - 1, :], ACT.Copy).then_inc(ohh_rdy, 1)

        def hgrn_dve_states(dve, link):
            lags = 0
            dve.wait_ge(ev_a, after(seg["h_f"])[1])
            dve.wait_ge(band_zero, 32)
            for d in range(CH):
                if d:
                    dve.wait_ge(prod_g, d)
                    dve.wait_ge(prod_v, d * (NG - 1))
                    nc.vector.tensor_tensor(by_chunk(scr1, 0, CH - d),
                                            by_chunk(kT if d == 1 else scr1, 0, CH - d),
                                            by_chunk(fT, d, CH - d), ALU.mult).then_inc(lag_rdy, 1)
                    dve.wait_ge(lag_rdy, d)
                for g in range(NG - 1):
                    if d:
                        dve.wait_ge(band_mm, (d - 1) * NG + g + 1)
                    c = slice(g * GROUP * NCH, (g + 1) * GROUP * NCH)
                    nc.vector.tensor_tensor(by_chunk(scr2, 0, CH - d)[:, c, :],
                                            by_chunk(scr1 if d else kT, 0, CH - d)[:, c, :],
                                            by_chunk(qT, d, CH - d)[:, c, :], ALU.mult).then_inc(prod_v, 1)
            dve.wait_ge(prod_g, CH)
            dve.wait_ge(prod_v, CH * (NG - 1))
            link(nc.vector.tensor_copy(by_chunk(scr1, 0, 1), by_chunk(fT, 0, 1)))
            for j in range(1, CH):
                link(nc.vector.tensor_tensor(by_chunk(scr1, j, 1), by_chunk(scr1, j - 1, 1),
                                             by_chunk(fT, j, 1), ALU.mult))
                if j == 4:
                    dve.wait_ge(band_mm, CH * NG)
                    nc.vector.tensor_copy(band[:, :], ps[:, 4, :]).then_inc(band_sb, 1)
                if j == 10:
                    dve.wait_ge(bandT_ps, 1)
                    nc.vector.tensor_copy(bandT[:, :, :].rearrange("p t n -> p (t n)"), ps[:, 5, :]
                                          ).then_inc(bandT_sb, 1)
            nc.vector.tensor_copy(decay[:, :, :].rearrange("p h c -> p (h c)"),
                                  by_chunk(scr1, CH - 1, 1).rearrange("p c j -> p (c j)")).then_inc(q_rdy, 1)
            nc.vector.tensor_tensor(qT[:, :, :].rearrange("p h t -> p (h t)"),
                                    qT[:, :, :].rearrange("p h t -> p (h t)"), scr1[:, :], ALU.mult
                                    ).then_inc(q_rdy, 1)
            dve.wait_ge(sx_rdy, CH)
            nc.vector.tensor_tensor(kT[:, :, :].rearrange("p h t -> p (h t)"),
                                    kT[:, :, :].rearrange("p h t -> p (h t)"), scr2[:, :], ALU.mult
                                    ).then_inc(k_rdy, 1)
            dve.wait_ge(hg_in, 32)
            dve.wait_ge(q_rdy, 2)
            for n in range(TT * 2):
                dve.wait_ge(kt_ps, n + 1)
                nc.vector.tensor_scalar(scr1[:, n * T:(n + 1) * T], ps[:, n % 4, :], evenodd[:, 0:1], None,
                                        ALU.mult).then_inc(ke_rdy, 1)
            for c in range(NCH - 1):
                dve.wait_ge(upd_ps, c + 1)
                if c:
                    dve.wait_ge(st_rdy, c)
                if c >= 2:
                    dve.wait_ge(outs_mm, c - 1)
                for h in range(NH):
                    u = ps[:, 2 + 4 * (c % 2) + h // 4, h % 4 * P:(h % 4 + 1) * P]
                    if c == 0:
                        ins = nc.vector.tensor_copy(state[:, 0, h, :], u)
                    else:
                        ins = nc.vector.scalar_tensor_tensor(
                            out=state[:, c % 2, h, :], in0=state[:, (c - 1) % 2, h, :],
                            scalar=decay[:, h, c:c + 1], in1=u, op0=ALU.mult, op1=ALU.add)
                ins.then_inc(st_rdy, 1)

        def hgrn_dve_out(dve, link):
            dve.wait_ge(ev_a, after(seg["h_g"])[1])
            r = ROWS["hgrn_out_norm"]

            def low(h):
                dve.wait_ge(ohh_rdy, h + 1)
                nc.vector.tensor_tensor(hl[:, h, :], gT[:, h, :], hh[:, h, :].bitcast(F32), ALU.subtract
                                        ).then_inc(ohl_rdy, 1)
            for h in range(NH):
                dve.wait_ge(ors_rdy, h + 1)
                link(nc.vector.scalar_tensor_tensor(out=kT[:, h, :], in0=kT[:, h, :], scalar=cols_b[:, r:r + 1],
                                                    in1=xn[:, h % 2, :], op0=ALU.mult, op1=ALU.mult))
                nc.vector.tensor_tensor(gT[:, h, :], gT[:, h, :], kT[:, h, :], ALU.mult).then_inc(og_rdy, 1)
                if h:
                    low(h - 1)
            low(NH - 1)

        def hgrn_pe_states(pe):
            pe.wait_ge(hg_in, 32)
            for d in range(CH):
                for g in range(NG):
                    if g == POOL_GROUP:
                        pe.wait_ge(prod_g, d + 1)
                    else:
                        pe.wait_ge(prod_v, d * (NG - 1) + g + 1)
                    for h in range(g * GROUP, (g + 1) * GROUP):
                        row = h * CH + d
                        m = nc.tensor.matmul(
                            ps[:, 4, :].rearrange("p (c j) -> p c j", j=CH)[:, :, 0:CH - d],
                            sel[:, P - 1 - row:2 * P - 1 - row],
                            by_chunk(scr2, 0, CH - d)[:, h * NCH:(h + 1) * NCH, :],
                            start=(d == 0 and h == 0), stop=(d == CH - 1 and h == NH - 1), skip_group_check=True)
                    m.then_inc(band_mm, 1)
            pe.wait_ge(band_sb, 1)
            for t in range(TT):
                m = nc.tensor.transpose(ps[:, 5, t * P:(t + 1) * P], band[:, t * P:(t + 1) * P], ident[:, :])
            m.then_inc(bandT_ps, 1)
            pe.wait_ge(k_rdy, 1)
            for n in range(2 * TT):
                if n >= 4:
                    pe.wait_ge(ke_rdy, n - 3)
                    pe.wait_ge(ko_rdy, n - 3)
                for i in range(4):
                    m = nc.tensor.transpose(ps[:, n % 4, i * P:(i + 1) * P],
                                            kT[:, 4 * (n % 2) + i, n // 2 * P:(n // 2 + 1) * P], ident[:, :])
                m.then_inc(kt_ps, 1)
            pe.wait_ge(ke_rdy, 2 * TT)
            pe.wait_ge(ko_rdy, 2 * TT)
            pe.wait_ge(ev_v, after(seg["h_v"])[2])
            pe.wait_ge(q_rdy, 2)
            for c in range(NCH):
                t, r = c // 8, c % 8
                rows = slice(32 * (r // 2), 32 * (r // 2) + 32)
                if c < NCH - 1:
                    if c >= 2:
                        pe.wait_ge(st_rdy, c - 1)
                    kx = scr1 if c % 2 == 0 else scr2
                    for h in range(NH):
                        m = nc.tensor.matmul(ps[:, 2 + 4 * (c % 2) + h // 4, h % 4 * P:(h % 4 + 1) * P],
                                             kx[rows, (t * NH + h) * P:(t * NH + h + 1) * P],
                                             vS[rows, t, h * P:(h + 1) * P], start=True, stop=True)
                    m.then_inc(upd_ps, 1)
                ob = 4 * (t % 2)
                if r == 0:
                    if t == 0:
                        pe.wait_ge(band_in, 16)
                    if t >= 2:
                        pe.wait_ge(o_rd, t - 1)
                    for h in range(NH):
                        nc.tensor.matmul(ps[:, ob + h // 4, h % 4 * P:(h % 4 + 1) * P],
                                         vS[:, t, h * P:(h + 1) * P],
                                         fT[:, :, :].rearrange("p h (x n) -> p (h x) n", n=P)[:, t * NH + h, :],
                                         start=(h % 4 == 0), stop=False, skip_group_check=True)
                if c:
                    pe.wait_ge(st_rdy, c)
                    for h in range(NH):
                        m = nc.tensor.matmul(
                            ps[:, ob + h // 4, h % 4 * P + r * CH:h % 4 * P + (r + 1) * CH],
                            state[:, (c - 1) % 2, h, :], qT[:, h, c * CH:(c + 1) * CH],
                            start=False, stop=(r == 7), skip_group_check=True)
                    m.then_inc(outs_mm, 1)
                    if r == 7:
                        pe.wait_ge(outs_mm, c)
                        pe.nop().then_inc(o_ps, 1)
            pe.wait_ge(st_rdy, NCH - 1)
            pe.wait_ge(o_rd, TT)

        def hgrn_pe_out(pe):
            for h in range(NH):
                pe.wait_ge(osq_rdy, h + 1)
                if h == 0:
                    boundary(pe, seg["h_out"]) if upto >= 4 else pe.wait_ge(ev_a, ea_end)
                if h >= 2:
                    pe.wait_ge(ors_rdy, h - 1)
                nc.tensor.matmul(ps[:, 2 + h % 2, :], ones[:, :], sq[:, h % 2, :], start=True, stop=True
                                 ).then_inc(oss_ps, 1)

        @block.sync
        def _(sp):
            w0 = a["ada_w"][0].rearrange("(k p) n -> p k n", p=P)
            for m in range(12):
                if m >= 6:
                    sp.wait_ge(ada0_used, m - 5)
                sp.dma_start(ada_first[:, m % 6, :].rearrange("p (k n) -> p k n", k=KT),
                             w0[:, :, m * 256:(m + 1) * 256]).then_inc(ada0_in[m % 6], 16)
            for s in segs:
                def load(b, par, more):
                    fixed = isinstance(b, int)
                    view = s.source(b, (lambda v: v) if fixed else sp.snap)
                    free = s.g0 + b - 1 if fixed else sp.snap(b + (s.g0 - 1))
                    if not fixed or free > 0:
                        sp.wait_ge(w_lo, free)
                    dst = raw[:, par, 0:s.ktiles * P * s.units if s.ktiles == 8 else s.ktiles * P]
                    if s.width == P and s.ktiles == 8:
                        dst = dst.rearrange("p (j k n) -> p j k n", j=2, k=s.ktiles)
                    else:
                        dst = dst.rearrange("p (k n) -> p k n", k=s.ktiles)
                    sp.dma_start(dst, view).then_inc(w_dma[par], 16)
                    for slot, count, tile in ada_slots(s, b, par):
                        w, first = s.ada[0].rearrange("(k p) n -> p k n", p=P), s.ada[1]
                        at = tile * P + first * P
                        if not fixed:
                            at, count = sp.snap(at), sp.snap(count - 1)
                        elif count >= 2:
                            count = count - 1
                        if not (fixed and count < 2 and s.ada0 == 0 and tile < 2):
                            sp.wait_ge(ada_used, count)
                        sp.dma_start(ada_ring[:, slot, :].rearrange("p (k n) -> p k n", k=KT),
                                     w[:, :, bass.ds(at, P)]).then_inc(ada_in[slot], 16)
                if s.name == "s_glu":
                    for b in range(s.n):
                        if b == 4:
                            s5_toeplitz(sp)
                        load(b, (s.g0 + b) % 2, True)
                else:
                    each_block(sp, s, load)
            sp.wait_ge(out_rdy, 2 * TT)
            sp.dma_start(out[0].rearrange("(t p) d -> p t d", p=P), xin[:, :, :]).then_inc(stored, 16)
            sp.wait_ge(stored, 16)

        @block.gpsimd
        def _(pool):
            nc.gpsimd.memset(zero_col[:, :], 0.0).then_inc(pool_set, 1)
            nc.gpsimd.memset(eps_col[:, :], EPS).then_inc(pool_set, 1)
            pool.wait_ge(cact_rdy, 1)
            ada_first_pool(pool)
            if upto >= 2:
                pool.wait_ge(mods_rdy, 1)
                nc.gpsimd.memset(scr2[:, 0:HEAD_SPAN // 8], 0.0).then_inc(pool_set, 1)
                for name in ("h_q", "h_f", "h_v"):
                    ada_sums(pool, seg[name])
            if upto >= 3:
                hgrn_pool(pool)
                for s in segs[3:]:
                    ada_sums(pool, s)
            if upto >= 6:
                pool.wait_ge(nsa_in, 32)
                nc.gpsimd.memset(vblk.rearrange("p g n -> p (g n)"), 0.0).then_inc(vblk0, 1)
                nc.gpsimd.memset(kcT[:, :, 31:32], 0.0).then_inc(vblk0, 1)
            if upto >= 11:
                s5_pool(pool)

        @block.scalar
        def _(act):
            links = [0]

            def link(ins):
                links[0] += 1
                ins.then_inc(a_link, 1)
                act.wait_ge(a_link, links[0])

            act.dma_start(vec_a[0:96, :], a["ada_b"].rearrange("l (c n) -> (l c) n", n=P)).then_inc(const_in, 16)
            act.dma_start(vec_a[96:112, :], a["kv_ada_b"].rearrange("(c n) -> c n", n=P)).then_inc(const_in, 16)
            act.dma_start(vec_a[112:120, :], a["c"].rearrange("o (c n) -> (o c) n", n=P)).then_inc(const_in, 16)
            act.dma_start(ident[:, :], a["k_ident"]).then_inc(const_in, 16)
            act.dma_start(ones[:, :], a["k_ones"]).then_inc(const_in, 16)
            for name, k, src in (
                    ("norm_mix", 16, a["norm_mix"].rearrange("l (c n) -> (l c) n", n=P)),
                    ("norm_ffn", 16, a["norm_ffn"].rearrange("l (c n) -> (l c) n", n=P)),
                    ("kv_norm", 8, a["kv_norm"].rearrange("(c n) -> c n", n=P)),
                    ("norm_mix_2", 16, a["norm_mix_2"].rearrange("l (c n) -> (l c) n", n=P)),
                    ("norm_ffn_2", 16, a["norm_ffn_2"].rearrange("l (c n) -> (l c) n", n=P)),
                    ("ssm_d_2", 8, a["ssm_d_2"].rearrange("l (c n) -> (l c) n", n=P)),
                    ("hgrn_out_norm", 1, a["hgrn_out_norm"]),
                    ("attn_subln_2", 1, a["attn_subln_2"]),
                    ("cmp_pos", 32, a["cmp_pos"].rearrange("b (m q) d -> (b m) (q d)", q=2))):
                r = ROWS[name]
                act.dma_start(vec_b[r:r + k, :], src).then_inc(const_in, 16)
            for h in range(2):
                c = slice(64 * h, 64 * h + 64)
                r = ROWS["gains"]
                act.dma_start(vec_b[r:r + 1, c], a["nsa_q_norm"]).then_inc(const_in, 16)
                act.dma_start(vec_b[r + 1:r + 4, c], a["nsa_k_norm"]).then_inc(const_in, 16)
                act.dma_start(vec_b[r + 4:r + 5, c], a["attn_q_gain_2"]).then_inc(const_in, 16)
                act.dma_start(vec_b[r + 5:r + 6, c], a["attn_k_gain_2"]).then_inc(const_in, 16)
            act.dma_start(xin[:, :, :], a["x"][0].rearrange("(t p) d -> p t d", p=P)).then_inc(x_in, 16)
            act.wait_ge(cols_rdy, 1)
            nc.scalar.activation(cact[:, :], cols_a[:, ROWS["c"]:ROWS["c"] + 8], ACT.Silu).then_inc(cact_rdy, 1)
            act.wait_ge(pool_set, 2)
            if upto >= 2:
                for ahead in range(2):
                    convert_hi(act, segs[0], 0, ahead, ahead)

            def norm(m, x_count):
                act.wait_ge(ev_v, x_count)
                for kt in range(0 if m in norm_after.values() else KT):
                    k = KT * m + kt
                    if k >= 2:
                        act.wait_ge(ssq_rdy, k - 1)
                    nc.scalar.activation(sq[:, k % 2, :], xT[:, kt, :], ACT.Square).then_inc(sq_rdy, 1)
                act.wait_ge(ssq_rdy, KT * m + KT)
                if m:
                    act.wait_ge(xn_rdy, KT * apply_of[m])
                link(nc.scalar.activation(rstd[:, :], ps[:, 7, :], ACT.Ln, scale=1.0 / D, bias=eps_col[:, :]))
                nc.scalar.activation(rstd[:, :], rstd[:, :], ACT.Exp, scale=-0.5).then_inc(rstd_rdy, 1)

            def apply(j, shift):
                for kt in range(KT):
                    k = KT * j + kt
                    act.wait_ge(xn_rdy, k + 1)
                    nc.scalar.activation(hh[:, kt, :], xn[:, k % 2, :], ACT.Identity,
                                         bias=zero_col[:, :] if shift is None else shift[:, kt:kt + 1]
                                         ).then_inc(hh_rdy, 1)

            def linear(s, evac):
                m = norm_after.get(s.name)

                def body(b, par, more):
                    evac(b, par)
                    if more:
                        convert_hi(act, s, b, par, 2)
                    if m is not None:
                        for j in range(s.dve):
                            act.wait_ge(ev_v, b * s.dve + (s.ev0 + j + 1))
                            act.wait_ge(ssq_rdy, b * s.dve + (KT * m + j - 1))
                            q = j if s.dve == 2 else (par + s.g0) % 2
                            nc.scalar.activation(sq[:, q:q + 1, :], xT[:, bass.ds(b * s.dve + j, 1), :], ACT.Square
                                                 ).then_inc(sq_rdy, 1)
                each_block(act, s, body)

            def none(b, par):
                pass

            def to_tile(s, func_dsts):
                def evac(b, par):
                    for j in range(2):
                        act.wait_ge(mm, b * 2 + (s.mm0 + j + 1))
                        for n, (func, dst, scale) in enumerate(func_dsts):
                            ins = nc.scalar.activation(dst[:, bass.ds(b * 2 + j, 1), :],
                                                       ps[:, 2 * par + j:2 * par + j + 1, :], func, scale=scale)
                        ins.then_inc(ev_a, 1)
                return evac

            if upto >= 2:
                act.wait_ge(mods_rdy, 1)
                act.wait_ge(pool_set, 3)
                for half in range(2):
                    act.dma_start(band_dram.ap().rearrange("m (ri n) -> (m ri) n", ri=8)[half * P:half * P + P, :],
                                  scr2[:, 0:HEAD_SPAN // 8]).then_inc(band_zero, 16)
                norm(0, FIRST_UNITS)
                apply(0, mod_cols(0)[1])
                linear(seg["h_q"], to_tile(seg["h_q"], [(ACT.Silu, qT, 1.0)]))
                linear(seg["h_f"], to_tile(seg["h_f"], [(ACT.Sigmoid, fT, 1.0), (ACT.Sigmoid, kT, -1.0)]))
                linear(seg["h_v"], none)
            if upto >= 3:
                hgrn_act_states(act)
                linear(seg["h_g"], to_tile(seg["h_g"], [(ACT.Silu, gT, 1.0)]))
                hgrn_act_out(act, link)
            if upto >= 4:
                linear(seg["h_out"], none)

            def ffn1_in(s):
                def evac(b, par):
                    act.wait_ge(mm, b * 2 + (s.mm0 + 1))
                    act.wait_ge(hidl_rdy, b + (hid0[s.name] - 1))
                    nc.scalar.activation(act_t[:, par, :], ps[:, 2 * par, :], ACT.Silu).then_inc(ev_a, 1)
                    act.wait_ge(ev_v, b + (s.ev0 + 1))
                    nc.scalar.activation(hid_h[:, bass.ds(b, 1), :], hid_f[:, par:par + 1, :], ACT.Copy
                                         ).then_inc(hidh_rdy, 1)
                return evac

            if upto >= 5:
                ffn_norm_act = lambda m, j, layer, x_count: (norm(m, x_count), apply(j, mod_cols(layer)[1]))
                ffn_norm_act(1, 1, 1, after(seg["h_out"])[2])
                for half in range(2):
                    linear(seg[f"ffn0_in{half}"], ffn1_in(seg[f"ffn0_in{half}"]))
                    linear(seg[f"ffn0_out{half}"], none)
            if upto >= 6:
                norm(2, after(seg["ffn0_out1"])[2])
                nsa_loads(act)
                apply(2, mod_cols("kv")[1])
                linear(seg["n_kvc"], to_tile(seg["n_kvc"], [(ACT.Copy, kvc, 1.0)]))
                linear(seg["n_ks"], to_tile(seg["n_ks"], [(ACT.Copy, ksr, 1.0)]))
                linear(seg["n_vs"], none)
                linear(seg["n_kw"], to_tile(seg["n_kw"], [(ACT.Copy, kwr, 1.0)]))
                linear(seg["n_vw"], none)
                apply(3, mod_cols(2)[1])
                linear(seg["n_q"], to_tile(seg["n_q"], [(ACT.Copy, nq, 1.0)]))
                nsa_act(act, link)
            if upto >= 7:
                linear(seg["n_out"], none)
            if upto >= 8:
                norm(3, after(seg["n_out"])[2])
                apply(4, mod_cols(3)[1])
                for half in range(2):
                    linear(seg[f"ffn1_in{half}"], ffn1_in(seg[f"ffn1_in{half}"]))
                    linear(seg[f"ffn1_out{half}"], none)
            if upto >= 9:
                norm(4, after(seg["ffn1_out1"])[2])
                act.dma_start(rope_c, a["k_rope"]).then_inc(dif_in, 16)
                act.dma_start(lam_vec, a["attn_lambda_2"].rearrange("o a b -> o (a b)").broadcast_to((P, 256))
                              ).then_inc(dif_in, 16)
                apply(5, None)
                linear(seg["d_q"], to_tile(seg["d_q"], [(ACT.Copy, dq, 1.0)]))
                linear(seg["d_k"], to_tile(seg["d_k"], [(ACT.Copy, dk, 1.0)]))
                linear(seg["d_v"], none)
                diff_act(act, link)
                linear(seg["d_out"], none)

            def mlp_in(s):
                def evac(b, par):
                    for j in range(2):
                        act.wait_ge(mm, b * 2 + (s.mm0 + j + 1))
                        act.wait_ge(hidl_rdy, b * 2 + (hid0[s.name] + j - 1))
                        nc.scalar.activation(act_t[:, j, :], ps[:, 2 * par + j, :], ACT.Relu).then_inc(ev_a, 1)
                    for j in range(2):
                        act.wait_ge(hidf_rdy, b * 2 + (squared0[s.name] + j + 1))
                        nc.scalar.activation(hid_h[:, bass.ds(b * 2 + j, 1), :], hid_f[:, j:j + 1, :], ACT.Copy
                                             ).then_inc(hidh_rdy, 1)
                return evac

            def mlp(layer, m, j, x_count):
                norm(m, x_count)
                apply(j, None)
                for half in range(2):
                    linear(seg[f"mlp{layer}_in{half}"], mlp_in(seg[f"mlp{layer}_in{half}"]))
                    linear(seg[f"mlp{layer}_out{half}"], none)

            if upto >= 10:
                mlp(0, 5, 6, after(seg["d_out"])[2])
            if upto >= 11:
                act.wait_ge(ev_v, seg["s_glu"].ev0)
                s5_loads(act)
                norm(6, seg["s_glu"].ev0)
                s5_act(act, link)

                def gate(b, par):
                    act.wait_ge(mm, b * 2 + (seg["s_glu"].mm0 + 2))
                    act.wait_ge(ev_v, b + (seg["s_glu"].ev0 - 1))
                    nc.scalar.activation(act_t[:, par, :], ps[:, 2 * par + 1, :], ACT.Sigmoid).then_inc(ev_a, 1)
                linear(seg["s_glu"], gate)
            if upto >= 12:
                mlp(1, 7, 8, after(seg["s_glu"])[2])

        @block.vector
        def _(dve):
            links = [0]

            def link(ins):
                links[0] += 1
                ins.then_inc(v_link, 1)
                dve.wait_ge(v_link, links[0])

            dve.nop().then_inc(hidl_rdy, 2)
            dve.wait_ge(cols_ps, 1)
            nc.vector.tensor_copy(cols_a[:, 0:NROW_A], ps[:, 6, 0:NROW_A]).then_inc(cols_rdy, 1)
            dve.wait_ge(cols_ps, 2)
            link(nc.vector.tensor_copy(cols_b[:, 0:NROW_B], ps[:, 7, 0:NROW_B]))
            for kt in range(KT):
                dve.wait_ge(mm, kt + 1)
                nc.vector.tensor_copy(xT[:, kt, :], ps[:, kt % 4, :]).then_inc(ev_v, 1)
            def modulated_gain(i, gain_row, at):
                return nc.vector.scalar_tensor_tensor(
                    out=gains_a[:, i, :], in0=mods[:, at:at + 8], scalar=1.0,
                    in1=cols_b[:, gain_row:gain_row + 8], op0=ALU.add, op1=ALU.mult)

            dve.wait_ge(cact_rdy, 1)
            ada_first_dve(dve)
            dve.wait_ge(ada0_used, 12)
            dve.wait_ge(cols_rdy, 1)
            link(nc.vector.tensor_tensor(mods[:, 0:24], ps[:, 5, 0:24], cols_a[:, 0:24], ALU.add))
            modulated_gain(0, ROWS["norm_mix"], 8).then_inc(mods_rdy, 1)
            if upto >= 2:
                for ahead in range(2):
                    convert_lo(dve, segs[0], 0, ahead, ahead)

            def apply(j, m, gain, shift, h_free):
                dve.wait_ge(rstd_rdy, m + 1)
                dve.wait_ge(mm, h_free)

                def low(k):
                    kt = k - KT * j
                    dve.wait_ge(hh_rdy, k + 1)
                    nc.vector.scalar_tensor_tensor(
                        out=hl[:, kt, :], in0=xn[:, k % 2, :],
                        scalar=0.0 if shift is None else shift[:, kt:kt + 1],
                        in1=hh[:, kt, :].bitcast(F32), op0=ALU.add, op1=ALU.subtract).then_inc(hl_rdy, 1)
                for kt in range(KT):
                    k = KT * j + kt
                    if k >= 2:
                        dve.wait_ge(hl_rdy, k - 1)
                    nc.vector.scalar_tensor_tensor(out=xn[:, k % 2, :], in0=xT[:, kt, :],
                                                   scalar=gain[:, kt:kt + 1], in1=rstd[:, :],
                                                   op0=ALU.mult, op1=ALU.mult).then_inc(xn_rdy, 1)
                    if kt:
                        low(k - 1)
                low(KT * j + KT - 1)

            def linear(s, evac):
                def body(b, par, more):
                    evac(b, par)
                    if more:
                        convert_lo(dve, s, b, par, 2)
                each_block(dve, s, body)
                ada_bias(dve, s)

            def none(b, par):
                pass

            def residual(s, gate):
                def evac(b, par):
                    for j in range(s.dve):
                        dve.wait_ge(mm, b * s.dve + (s.mm0 + j + 1))
                        kt = b * s.dve + j
                        x = xT[:, bass.ds(kt, 1), :]
                        p = ps[:, 2 * par + j:2 * par + j + 1, :]
                        if gate is None:
                            nc.vector.tensor_tensor(x, x, p, ALU.add).then_inc(ev_v, 1)
                        else:
                            nc.vector.scalar_tensor_tensor(out=x, in0=p, scalar=gate[:, bass.ds(kt, 1)],
                                                           in1=x, op0=ALU.mult, op1=ALU.add).then_inc(ev_v, 1)
                return evac

            def to_token_major(s, dst, cols=256):
                def evac(b, par):
                    for j in range(2):
                        dve.wait_ge(mm, b * 2 + (s.mm0 + j + 1))
                        nc.vector.tensor_copy(
                            dst[:, 2 * j:2 * j + 2, bass.ds(b * cols, cols)],
                            ps[:, 2 * par + j, :].rearrange("p (t n) -> p t n", t=2)).then_inc(ev_v, 1)
                return evac

            if upto >= 2:
                apply(0, 0, *mod_cols(0), FIRST_UNITS)
                linear(seg["h_q"], none)
                linear(seg["h_f"], none)
                linear(seg["h_v"], to_token_major(seg["h_v"], vS))
            if upto >= 3:
                hgrn_dve_states(dve, link)
                linear(seg["h_g"], none)
                hgrn_dve_out(dve, link)
            if upto >= 4:
                linear(seg["h_out"], residual(seg["h_out"], mods[:, 16:24]))

            def ffn1_in(s):
                def evac(b, par):
                    dve.wait_ge(mm, b * 2 + (s.mm0 + 2))
                    dve.wait_ge(ev_a, b + (s.ea0 + 1))
                    dve.wait_ge(hidl_rdy, b + (hid0[s.name] - 1))
                    nc.vector.tensor_tensor(hid_f[:, par, :], act_t[:, par, :], ps[:, 2 * par + 1, :],
                                            ALU.mult).then_inc(ev_v, 1)
                    dve.wait_ge(ev_v, b + (s.ev0 + 1))
                    dve.wait_ge(hidh_rdy, b + (hid0[s.name] - 1))
                    nc.vector.tensor_tensor(hid_l[:, bass.ds(b, 1), :], hid_f[:, par:par + 1, :],
                                            hid_h[:, bass.ds(b, 1), :].bitcast(F32), ALU.subtract
                                            ).then_inc(hidl_rdy, 1)
                return evac

            if upto >= 5:
                link(modulated_gain(1, ROWS["norm_ffn"], 32))
                apply(1, 1, *mod_cols(1), after(seg["h_out"])[0])
                for half in range(2):
                    linear(seg[f"ffn0_in{half}"], ffn1_in(seg[f"ffn0_in{half}"]))
                    linear(seg[f"ffn0_out{half}"], residual(seg[f"ffn0_out{half}"], mods[:, 40:48]))

            if upto >= 6:
                link(modulated_gain(6, ROWS["kv_norm"], 104))
                link(modulated_gain(2, ROWS["norm_mix"] + 8, 56))
                apply(2, 2, *mod_cols("kv"), after(seg["ffn0_out1"])[0])
                for name in ("n_kvc", "n_ks"):
                    linear(seg[name], none)
                linear(seg["n_vs"], to_token_major(seg["n_vs"], v_sel))
                linear(seg["n_kw"], none)
                linear(seg["n_vw"], to_token_major(seg["n_vw"], v_win))
                apply(3, 2, *mod_cols(2), after(seg["n_vw"])[0])
                linear(seg["n_q"], none)
                nsa_dve(dve, link)
            if upto >= 7:
                linear(seg["n_out"], residual(seg["n_out"], mods[:, 64:72]))
            if upto >= 8:
                link(modulated_gain(3, ROWS["norm_ffn"] + 8, 80))
                apply(4, 3, *mod_cols(3), after(seg["n_out"])[0])
                for half in range(2):
                    linear(seg[f"ffn1_in{half}"], ffn1_in(seg[f"ffn1_in{half}"]))
                    linear(seg[f"ffn1_out{half}"], residual(seg[f"ffn1_out{half}"], mods[:, 88:96]))
            if upto >= 9:
                r = ROWS["norm_mix_2"]
                apply(5, 4, cols_b[:, r:r + 8], None, after(seg["ffn1_out1"])[0])
                linear(seg["d_q"], none)
                linear(seg["d_k"], none)
                linear(seg["d_v"], to_token_major(seg["d_v"], dv))
                diff_dve(dve, link)
                linear(seg["d_out"], residual(seg["d_out"], None))

            def mlp_in(s):
                def evac(b, par):
                    for j in range(2):
                        dve.wait_ge(ev_a, b * 2 + (s.ea0 + j + 1))
                        nc.vector.tensor_tensor(hid_f[:, j, :], act_t[:, j, :], act_t[:, j, :], ALU.mult
                                                ).then_inc(hidf_rdy, 1)
                    for j in range(2):
                        dve.wait_ge(hidh_rdy, b * 2 + (hid0[s.name] + j - 1))
                        nc.vector.tensor_tensor(hid_l[:, bass.ds(b * 2 + j, 1), :], hid_f[:, j:j + 1, :],
                                                hid_h[:, bass.ds(b * 2 + j, 1), :].bitcast(F32), ALU.subtract
                                                ).then_inc(hidl_rdy, 1)
                return evac

            def mlp(layer, m, j, h_free):
                r = ROWS["norm_ffn_2"] + 8 * layer
                apply(j, m, cols_b[:, r:r + 8], None, h_free)
                for half in range(2):
                    linear(seg[f"mlp{layer}_in{half}"], mlp_in(seg[f"mlp{layer}_in{half}"]))
                    linear(seg[f"mlp{layer}_out{half}"], residual(seg[f"mlp{layer}_out{half}"], None))

            if upto >= 10:
                mlp(0, 5, 6, after(seg["d_out"])[0])
            if upto >= 11:
                s5_dve(dve, link)

                def glu(b, par):
                    dve.wait_ge(mm, b * 2 + (seg["s_glu"].mm0 + 1))
                    dve.wait_ge(ev_a, b + (seg["s_glu"].ea0 + 1))
                    nc.vector.tensor_tensor(hid_f[:, par, :], act_t[:, par, :], ps[:, 2 * par, :], ALU.mult
                                            ).then_inc(glu_rdy, 1)
                    dve.wait_ge(glu_rdy, b + 1)
                    x = xT[:, bass.ds(b, 1), :]
                    nc.vector.tensor_tensor(x, x, hid_f[:, par:par + 1, :], ALU.add).then_inc(ev_v, 1)
                linear(seg["s_glu"], glu)
            if upto >= 12:
                mlp(1, 7, 8, after(seg["s_glu"])[0])

            for n in range(2 * TT):
                dve.wait_ge(out_ps, n + 1)
                nc.vector.tensor_copy(xin[:, n // 2, n % 2 * T:(n % 2 + 1) * T], ps[:, n % 4, :]
                                      ).then_inc(out_rdy, 1)

        @block.tensor
        def _(pe):
            pe.wait_ge(const_in, 16 * 22)
            nc.tensor.transpose(ps[:, 6, 0:NROW_A], vec_a[0:NROW_A, :], ident[0:NROW_A, 0:NROW_A]).then_inc(cols_ps, 1)
            nc.tensor.transpose(ps[:, 7, 0:NROW_B], vec_b[0:NROW_B, :], ident[0:NROW_B, 0:NROW_B]
                                ).then_inc(cols_ps, 1)
            pe.wait_ge(x_in, 16)
            for kt in range(KT):
                if kt >= 4:
                    pe.wait_ge(ev_v, kt - 3)
                for t in range(TT):
                    m = nc.tensor.transpose(ps[:, kt % 4, t * P:(t + 1) * P], xin[:, t, kt * P:(kt + 1) * P],
                                            ident[:, :])
                m.then_inc(mm, 1)

            for m in range(12):
                if m in DVE_FIRST:
                    pe.wait_ge(ada0_sum_v, KT * (DVE_FIRST.index(m) + 1))
                else:
                    pe.wait_ge(ada0_sum_g, 4 * (POOL_FIRST.index(m) + 1))
                for j in range(2):
                    mt = nc.tensor.matmul(ps[:, 5, 2 * m + j:2 * m + j + 1],
                                          ada_first[:, m % 6, j * P:(j + 1) * P], ones[:, 0:1],
                                          start=True, stop=True)
                mt.then_inc(ada0_used, 1)

            def square_sums(s, m, b, par):
                for j in range(s.dve):
                    kt = b * s.dve + j
                    first = isinstance(kt, int) and kt == 0
                    if first:
                        pe.wait_ge(rstd_rdy, m)
                    pe.wait_ge(sq_rdy, kt + (KT * m + 1))
                    q = j if s.dve == 2 else (par + s.g0) % 2
                    nc.tensor.matmul(ps[:, 7, :], ones[:, :], sq[:, q, :], start=first,
                                     stop=isinstance(kt, int) and kt == KT - 1).then_inc(ssq_rdy, 1)

            def norm(m):
                for kt in range(0 if m in norm_after.values() else KT):
                    k = KT * m + kt
                    pe.wait_ge(sq_rdy, k + 1)
                    if m and kt == 0:
                        pe.wait_ge(rstd_rdy, m)
                    nc.tensor.matmul(ps[:, 7, :], ones[:, :], sq[:, k % 2, :], start=(kt == 0),
                                     stop=(kt == KT - 1)).then_inc(ssq_rdy, 1)

            def linear(s, hi=hh, lo=hl, token_major=False, need=None):
                prev = segs[segs.index(s) - 1] if s.g0 else None
                if prev is not None and (prev.act, prev.dve) != (s.act, s.dve):
                    boundary(pe, s)

                if s.ada and s.ada_seg >= 2:
                    pe.wait_ge(ada_rdy, s.ada_seg - 1)

                def body(b, par, more):
                    first = isinstance(b, int) and b == 0
                    weight_products(pe, s, b, par, hi, lo, token_major, need if first else None)
                    ada_products(pe, s, b, par)
                    if m is not None and not first:
                        square_sums(s, m, b - 1, 1 - par)
                m = norm_after.get(s.name)
                each_block(pe, s, body, need is not None or m is not None)
                if m is not None:
                    square_sums(s, m, s.n - 1, (s.g0 + s.n - 1) % 2)

            if upto >= 2:
                norm(0)
                linear(seg["h_q"], need=0)
                linear(seg["h_f"])
                linear(seg["h_v"], token_major=True)
            if upto >= 3:
                hgrn_pe_states(pe)
                linear(seg["h_g"])
                hgrn_pe_out(pe)
            if upto >= 4:
                pe.wait_ge(ohl_rdy, NH)
                linear(seg["h_out"])
            if upto >= 5:
                norm(1)
                for half in range(2):
                    linear(seg[f"ffn0_in{half}"], need=KT if half == 0 else None)
                    pe.wait_ge(hidl_rdy, hid0[f"ffn0_in{half}"] + 11)
                    linear(seg[f"ffn0_out{half}"], hid_h, hid_l)

            if upto >= 6:
                norm(2)
                linear(seg["n_kvc"], need=2 * KT)
                linear(seg["n_ks"])
                linear(seg["n_vs"], token_major=True)
                linear(seg["n_kw"])
                linear(seg["n_vw"], token_major=True)
                linear(seg["n_q"], need=3 * KT)
                nsa_pe(pe)
            if upto >= 7:
                pe.wait_ge(ot_l, KT)
                linear(seg["n_out"])
            if upto >= 8:
                norm(3)
                for half in range(2):
                    linear(seg[f"ffn1_in{half}"], need=4 * KT if half == 0 else None)
                    pe.wait_ge(hidl_rdy, hid0[f"ffn1_in{half}"] + 11)
                    linear(seg[f"ffn1_out{half}"], hid_h, hid_l)
            if upto >= 9:
                norm(4)
                linear(seg["d_q"], need=5 * KT)
                linear(seg["d_k"])
                linear(seg["d_v"], token_major=True)
                diff_pe(pe)
                linear(seg["d_out"])

            def mlp(layer, m, j):
                norm(m)
                for half in range(2):
                    linear(seg[f"mlp{layer}_in{half}"], need=j * KT if half == 0 else None)
                    pe.wait_ge(hidl_rdy, hid0[f"mlp{layer}_in{half}"] + 16)
                    linear(seg[f"mlp{layer}_out{half}"], hid_h, hid_l)

            if upto >= 10:
                mlp(0, 5, 6)
            if upto >= 11:
                norm(6)
                s5_pe(pe)
                linear(seg["s_glu"], need=KT * K5)
            if upto >= 12:
                mlp(1, 7, 8)

            pe.wait_ge(ev_v, ev_end)
            if ea_end:
                pe.wait_ge(ev_a, ea_end)
            for n in range(2 * TT):
                if n >= 4:
                    pe.wait_ge(out_rdy, n - 3)
                for i in range(4):
                    kt = 4 * (n % 2) + i
                    m = nc.tensor.transpose(ps[:, n % 4, i * P:(i + 1) * P], xT[:, kt, n // 2 * P:(n // 2 + 1) * P],
                                            ident[:, :])
                m.then_inc(out_ps, 1)


_INS = ["x", "c", "ada_w", "ada_b", "norm_mix", "norm_ffn", "hgrn_w_in", "hgrn_out_norm", "hgrn_w_out",
        "kv_ada_w", "kv_ada_b", "kv_norm", "nsa_w_kv", "nsa_k_norm", "cmp_pos", "cmp_w1", "cmp_w2",
        "nsa_w_q", "nsa_q_norm", "nsa_w_out", "ffn_w_in", "ffn_w_out", "norm_mix_2", "norm_ffn_2",
        "attn_w_qkv_2", "attn_q_gain_2", "attn_k_gain_2", "attn_lambda_2", "attn_subln_2", "attn_w_o_2",
        "ssm_a_re_2", "ssm_a_im_2", "ssm_log_dt_2", "ssm_b_re_2", "ssm_b_im_2", "ssm_c_re_2", "ssm_c_im_2",
        "ssm_d_2", "ssm_w_glu_2", "ffn_w_up_2", "ffn_w_down_2"]


def constants():
    f = np.float32
    p = np.arange(P)
    odd = (p // CH) % 2
    sel = np.zeros((P, 2 * P - 1), f)
    sel[:, P - 1] = 1
    inv = 1.0 / (np.float32(10000.0) ** (np.arange(0, 64, 2, dtype=f) / f(64)))
    ang = (np.arange(T, dtype=f)[:, None] * inv.astype(f)[None, :]).astype(f)
    cos, sin = np.cos(ang).T[p % 32], np.sin(ang).T[p % 32]
    rot = np.zeros((P, P), f)
    low = p % 64 < 32
    rot[(p + 32)[low], p[low]] = -1
    rot[(p - 32)[~low], p[~low]] = 1
    same = (p[:, None] // 64 == p[None, :] // 64).astype(f)
    rope = np.concatenate([cos, sin, rot, same], 1).astype(f)
    dup = [np.eye(P, dtype=f)[:, 64 * i + p % 64] for i in range(2)]
    rotdup = [rot[:, 64 * i + p % 64] for i in range(2)]
    causal = np.where(p[None, :] <= p[:, None], 0, NEG)
    t = np.arange(T).reshape(TT, P)
    ends = np.where(np.arange(32) < 31, np.arange(32) * 16 + 31, T)
    cmpm = np.concatenate([np.where(ends[None, :] <= t[i][:, None], 0, NEG) for i in range(TT)], 1)
    nsa = np.concatenate(dup + rotdup + [causal, cmpm, (t >= 31).T], 1).astype(f)
    return {
        "k_ident": np.eye(P, dtype=f),
        "k_ones": np.ones((P, P), f),
        "k_sel": sel,
        "k_evenodd": np.stack([1 - odd, odd], 1).astype(f),
        "k_rope": rope,
        "k_nsa": nsa,
    }


def kernel(_upto=99, **inputs):
    import concourse.bacc as _bacc
    from concourse.bass_utils import run_bass_kernel_spmd as _run

    nc = _bacc.Bacc("TRN2", target_bir_lowering=False, num_devices=1, dynamic_dma_scratch_size=1024)
    arrays, aps = {}, {}
    for name, value in [(n, inputs[n]) for n in _INS] + list(constants().items()):
        value = np.ascontiguousarray(value)
        arrays[f"in_{name}"] = value
        aps[name] = nc.dram_tensor(f"in_{name}", value.shape, mybir.dt.from_np(value.dtype),
                                   kind="ExternalInput").ap()
    out = nc.dram_tensor("out_0", (1, T, D), F32, kind="ExternalOutput").ap()
    build(nc, aps, out, _upto)
    result = _run(nc, [arrays], core_ids=[0])
    return result.results[0]["out_0"]
```
